# Optimizing a Trainium2 kernel written in Bass

```python
import jax, jax.numpy as jnp
from jax import lax
import numpy as np
import math

D_MODEL = 2048
BATCH = 1
SEQ = 256
DEPTH = 1

D_MIX = D_MODEL
HG_DK = 128
HG_DV = 128
HG_WIDTH = D_MIX // 2
HG_HEADS = HG_WIDTH // HG_DV
HG_QK = HG_HEADS * HG_DK
GDN_DK = 128
GDN_DV = 128
GDN_WIDTH = D_MIX - HG_WIDTH
GDN_HEADS = GDN_WIDTH // GDN_DV
GDN_QK = GDN_HEADS * GDN_DK
CONV_K = 4
CHUNK = 64
D_FF = 4 * D_MODEL
N_MOD = 6
EPS = 1e-6

HG_COLS = 2 * HG_QK + 2 * HG_WIDTH
GDN_CONV_CH = 2 * GDN_QK + GDN_WIDTH
GDN_COLS = GDN_CONV_CH + GDN_WIDTH + 2 * GDN_HEADS
IN_COLS = HG_COLS + GDN_COLS


def rmsnorm(x, w):
    x32 = x.astype(jnp.float32)
    y = x32 * lax.rsqrt(jnp.mean(x32 * x32, axis=-1, keepdims=True) + EPS)
    return (y * w.astype(jnp.float32)).astype(x.dtype)

def l2norm(x):
    return x * lax.rsqrt(jnp.sum(x * x, axis=-1, keepdims=True) + EPS)

def to_chunks(x):
    B, T, H, D = x.shape
    return x.reshape(B, T // CHUNK, CHUNK, H, D).transpose(1, 0, 3, 2, 4)

def from_chunks(x):
    N, B, H, C, D = x.shape
    return x.transpose(1, 0, 3, 2, 4).reshape(B, N * C, H, D)

def causal_conv(u, w):
    ch = u.shape[-1]
    return lax.conv_general_dilated(
        u, w[:, None, :].astype(u.dtype), window_strides=(1,), padding=[(CONV_K - 1, 0)],
        dimension_numbers=('NWC', 'WIO', 'NWC'), feature_group_count=ch)

def hgrn2_chunked(q, log_f, k, v):
    B, T, H, DK = q.shape
    DV = v.shape[-1]
    causal = jnp.tril(jnp.ones((CHUNK, CHUNK), dtype=bool))

    def step(S, xs):
        qc, lfc, kc, vc = xs
        b = jnp.cumsum(lfc, axis=-2)
        diff = b[:, :, :, None, :] - b[:, :, None, :, :]
        decay = jnp.exp(jnp.where(causal[None, None, :, :, None], diff, -jnp.inf))
        attn = jnp.einsum('bhtk,bhsk,bhtsk->bhts', qc, kc, decay)
        o = (jnp.einsum('bhts,bhsv->bhtv', attn, vc)
             + jnp.einsum('bhtk,bhkv->bhtv', qc * jnp.exp(b), S))
        b_last = b[:, :, -1:, :]
        S_new = (S * jnp.exp(b_last[:, :, 0, :, None])
                 + jnp.einsum('bhsk,bhsv->bhkv', kc * jnp.exp(b_last - b), vc))
        return S_new, o

    S0 = jnp.zeros((B, H, DK, DV), jnp.float32)
    _, o = lax.scan(step, S0, (to_chunks(q), to_chunks(log_f), to_chunks(k), to_chunks(v)))
    return from_chunks(o)

def gated_delta_chunked(q, k, v, log_a, beta):
    B, T, H, DK = q.shape
    DV = v.shape[-1]
    qc, kc, vc = to_chunks(q), to_chunks(k), to_chunks(v)
    g = jnp.cumsum(to_chunks(log_a[..., None])[..., 0], axis=-1)
    bc = to_chunks(beta[..., None])[..., 0]
    incl = jnp.tril(jnp.ones((CHUNK, CHUNK), dtype=bool))
    strict = jnp.tril(jnp.ones((CHUNK, CHUNK), dtype=bool), -1)
    gamma = jnp.exp(jnp.where(incl, g[..., :, None] - g[..., None, :], -jnp.inf))
    kk = jnp.einsum('nbhtk,nbhsk->nbhts', kc, kc)
    m = jnp.where(strict, bc[..., :, None] * kk * gamma, 0.0)
    a_mat = jnp.eye(CHUNK, dtype=jnp.float32) + m
    rhs = jnp.concatenate([vc * bc[..., None], kc * (bc * jnp.exp(g))[..., None]], axis=-1)
    sol = lax.linalg.triangular_solve(a_mat, rhs, left_side=True, lower=True, unit_diagonal=True)
    u, w = sol[..., :DV], sol[..., DV:]
    qk = jnp.einsum('nbhtk,nbhsk->nbhts', qc, kc) * gamma
    q_dec = qc * jnp.exp(g)[..., None]
    k_tail = kc * jnp.exp(g[..., -1:] - g)[..., None]
    tail = jnp.exp(g[..., -1])

    def step(S, xs):
        u_c, w_c, qk_c, qd_c, kt_c, tl_c = xs
        v_new = u_c - jnp.einsum('bhck,bhkv->bhcv', w_c, S)
        o = jnp.einsum('bhck,bhkv->bhcv', qd_c, S) + jnp.einsum('bhts,bhsv->bhtv', qk_c, v_new)
        S = S * tl_c[..., None, None] + jnp.einsum('bhck,bhcv->bhkv', kt_c, v_new)
        return S, o

    S0 = jnp.zeros((B, H, DK, DV), jnp.float32)
    _, o = lax.scan(step, S0, (u, w, qk, q_dec, k_tail, tail))
    return from_chunks(o)

def hgrn2_group(p, lb, norm_w):
    B, T, _ = p.shape
    dt = p.dtype
    p32 = p.astype(jnp.float32)
    q = p32[..., :HG_QK].reshape(B, T, HG_HEADS, HG_DK)
    f_logit = p32[..., HG_QK:2 * HG_QK].reshape(B, T, HG_HEADS, HG_DK)
    i_in = p32[..., 2 * HG_QK:2 * HG_QK + HG_WIDTH].reshape(B, T, HG_HEADS, HG_DV)
    g_out = p[..., 2 * HG_QK + HG_WIDTH:].reshape(B, T, HG_HEADS, HG_DV)
    f = lb + (1.0 - lb) * jax.nn.sigmoid(f_logit)
    o = hgrn2_chunked(q, jnp.log(f), 1.0 - f, i_in).astype(dt)
    o = rmsnorm(o, norm_w) * jax.nn.silu(g_out)
    return o.reshape(B, T, HG_WIDTH)

def gdn_group(p, conv_w, a_log, dt_bias, norm_w):
    B, T, _ = p.shape
    dt = p.dtype
    qkv = jax.nn.silu(causal_conv(p[..., :GDN_CONV_CH], conv_w)).astype(jnp.float32)
    q = l2norm(qkv[..., :GDN_QK].reshape(B, T, GDN_HEADS, GDN_DK)) * (GDN_DK ** -0.5)
    k = l2norm(qkv[..., GDN_QK:2 * GDN_QK].reshape(B, T, GDN_HEADS, GDN_DK))
    v = qkv[..., 2 * GDN_QK:].reshape(B, T, GDN_HEADS, GDN_DV)
    off = GDN_CONV_CH
    g_out = p[..., off:off + GDN_WIDTH].reshape(B, T, GDN_HEADS, GDN_DV)
    a = p[..., off + GDN_WIDTH:off + GDN_WIDTH + GDN_HEADS].astype(jnp.float32)
    b = p[..., off + GDN_WIDTH + GDN_HEADS:].astype(jnp.float32)
    log_a = -jnp.exp(a_log.astype(jnp.float32)) * jax.nn.softplus(a + dt_bias.astype(jnp.float32))
    beta = jax.nn.sigmoid(b)
    o = gated_delta_chunked(q, k, v, log_a, beta).astype(dt)
    o = rmsnorm(o, norm_w) * jax.nn.silu(g_out)
    return o.reshape(B, T, GDN_WIDTH)

def first_inputs(seed: int = 0) -> dict:
    key = jax.random.key(seed)
    ks = jax.random.split(key, 20)
    f32 = jnp.float32
    nrm = lambda k, s, sc: jax.random.normal(k, s, f32) * sc
    gain = lambda k, s: 1.0 + 0.05 * jax.random.normal(k, s, f32)
    dtv = jnp.exp(jax.random.uniform(ks[13], (DEPTH, GDN_HEADS), f32, np.log(1e-3), np.log(1e-1)))
    return {
        "x": nrm(ks[0], (BATCH, SEQ, D_MODEL), 1.0),
        "c": nrm(ks[1], (BATCH, D_MODEL), 1.0),
        "w_ada": nrm(ks[2], (DEPTH, D_MODEL, N_MOD * D_MODEL), 0.5 * D_MODEL ** -0.5),
        "b_ada": nrm(ks[3], (DEPTH, N_MOD * D_MODEL), 0.02),
        "pre_mix_norm": gain(ks[4], (DEPTH, D_MODEL)),
        "post_mix_norm": gain(ks[5], (DEPTH, D_MODEL)),
        "pre_ffn_norm": gain(ks[6], (DEPTH, D_MODEL)),
        "post_ffn_norm": gain(ks[7], (DEPTH, D_MODEL)),
        "w_in": nrm(ks[8], (DEPTH, D_MODEL, IN_COLS), D_MODEL ** -0.5),
        "hg_lb_logits": nrm(ks[9], (DEPTH + 1, HG_HEADS, HG_DK), 0.5),
        "hg_norm": gain(ks[10], (DEPTH, HG_DV)),
        "gdn_conv_w": nrm(ks[11], (DEPTH, CONV_K, GDN_CONV_CH), CONV_K ** -0.5),
        "gdn_a_log": jnp.log(jax.random.uniform(ks[12], (DEPTH, GDN_HEADS), f32, 1.0, 16.0)),
        "gdn_dt_bias": dtv + jnp.log(-jnp.expm1(-dtv)),
        "gdn_norm": gain(ks[14], (DEPTH, GDN_DV)),
        "w_out": nrm(ks[15], (DEPTH, D_MIX, D_MODEL), D_MIX ** -0.5),
        "w_ff1": nrm(ks[16], (DEPTH, D_MODEL, D_FF), D_MODEL ** -0.5),
        "w_ff2": nrm(ks[17], (DEPTH, D_FF, D_MODEL), D_FF ** -0.5),
    }

def first_block(x, c, w_ada, b_ada, pre_mix_norm, post_mix_norm, pre_ffn_norm, post_ffn_norm,
              w_in, hg_lb_logits, hg_norm, gdn_conv_w, gdn_a_log, gdn_dt_bias, gdn_norm,
              w_out, w_ff1, w_ff2):
    lb_all = jnp.cumsum(jax.nn.softmax(hg_lb_logits.astype(jnp.float32), axis=0), axis=0)
    c_act = jax.nn.silu(c)
    for l in range(DEPTH):
        mod = c_act @ w_ada[l] + b_ada[l]
        sh_m, sc_m, gt_m, sh_f, sc_f, gt_f = jnp.split(mod[:, None, :], N_MOD, axis=-1)
        h = rmsnorm(x, pre_mix_norm[l]) * (1.0 + sc_m) + sh_m
        proj = h @ w_in[l]
        o_hg = hgrn2_group(proj[..., :HG_COLS], lb_all[l], hg_norm[l])
        o_gdn = gdn_group(proj[..., HG_COLS:], gdn_conv_w[l], gdn_a_log[l], gdn_dt_bias[l], gdn_norm[l])
        y = jnp.concatenate([o_hg, o_gdn], axis=-1) @ w_out[l]
        x = x + gt_m * rmsnorm(y, post_mix_norm[l])
        h = rmsnorm(x, pre_ffn_norm[l]) * (1.0 + sc_f) + sh_f
        y = jnp.square(jax.nn.relu(h @ w_ff1[l])) @ w_ff2[l]
        x = x + gt_f * rmsnorm(y, post_ffn_norm[l])
    return x


MEM_LEN = 256
HEAD_DIM = 64
A_WIDTH = 3 * D_MODEL // 8
A_HEADS = A_WIDTH // HEAD_DIM
A_PATTERNS = ((128, 1), (512, 4), (2048, 16))
B_WIDTH = D_MODEL // 4
B_HEADS = B_WIDTH // HEAD_DIM
BLOCK_Q = 128
C_HEADS = 4
C_VW = 3 * D_MODEL // 8
C_DV = C_VW // C_HEADS
C_DK = C_DV // 2
C_KW = C_HEADS * C_DK
C_GATE_RANK = 16
C_GATE_TAU = 16.0
C_CHUNK = 64
MIX_WIDTH = A_WIDTH + B_WIDTH + C_VW
PROJ_SPLITS = (A_WIDTH, A_WIDTH, A_WIDTH, B_WIDTH, B_WIDTH, B_WIDTH, B_HEADS, C_KW, C_KW, C_VW, C_VW, C_GATE_RANK)
PROJ_WIDTH = sum(PROJ_SPLITS)
CROSS_HEADS = 4
CROSS_DH = 128
CROSS_WIDTH = CROSS_HEADS * CROSS_DH
D_FF_2 = ((8 * D_MODEL // 3 + 127) // 128) * 128
CONV_W = 3
REL_BUCKETS = 32
REL_MAX_DIST = 2048


def rms_norm(x, g):
    xf = x.astype(jnp.float32)
    y = xf * lax.rsqrt(jnp.mean(xf * xf, axis=-1, keepdims=True) + EPS)
    return (y * g.astype(jnp.float32)).astype(x.dtype)

def t5_bucket(dist):
    max_exact = REL_BUCKETS // 2
    d = np.maximum(dist, 1).astype(np.float32)
    large = max_exact + (np.log(d / max_exact) / math.log(REL_MAX_DIST / max_exact)
                         * (REL_BUCKETS - max_exact)).astype(np.int32)
    return np.where(dist < max_exact, dist, np.minimum(large, REL_BUCKETS - 1)).astype(np.int32)

def dilated_pattern(q, k, v, rel_table, window, dilation):
    B, S, H, Dh = q.shape
    span = window // dilation
    L = S // dilation
    nb = -(-L // span)
    Lp = nb * span

    def classes(t):
        t = t.reshape(B, L, dilation, H, Dh).transpose(0, 3, 2, 1, 4)
        return jnp.pad(t, ((0, 0), (0, 0), (0, 0), (0, Lp - L), (0, 0)))

    def band(t):
        t = jnp.pad(classes(t), ((0, 0), (0, 0), (0, 0), (span, 0), (0, 0)))
        t = t.reshape(B, H, dilation, nb + 1, span, Dh)
        return jnp.concatenate([t[:, :, :, :-1], t[:, :, :, 1:]], axis=4)

    qb = classes(q).reshape(B, H, dilation, nb, span, Dh)
    kb, vb = band(k), band(v)
    i = np.arange(span)[:, None]
    j = np.arange(2 * span)[None, :]
    step = i + span - j
    valid = (step >= 0) & (step <= span) & (np.arange(nb)[:, None, None] * span + j - span >= 0)
    bias = rel_table[t5_bucket(np.clip(step, 0, span) * dilation)]
    bias = jnp.transpose(bias, (2, 0, 1)).astype(jnp.float32)
    logits = jnp.einsum('bhrnid,bhrnjd->bhrnij', qb, kb,
                        preferred_element_type=jnp.float32) * HEAD_DIM ** -0.5
    logits = jnp.where(valid, logits + bias[None, :, None, None], -jnp.inf)
    m = jnp.max(logits, axis=-1, keepdims=True)
    p = jnp.exp(logits - m)
    s = jnp.sum(p, axis=-1, keepdims=True)
    o = jnp.einsum('bhrnij,bhrnjd->bhrnid', p.astype(v.dtype), vb,
                   preferred_element_type=jnp.float32) / s
    lse = (m + jnp.log(s))[..., 0]
    o = o.reshape(B, H, dilation, Lp, Dh)[:, :, :, :L].transpose(0, 3, 2, 1, 4).reshape(B, S, H, Dh)
    lse = lse.reshape(B, H, dilation, Lp)[:, :, :, :L].transpose(0, 3, 2, 1).reshape(B, S, H)
    return o, lse

def dilated_mixture_attention(q, k, v, rel_table):
    outs, lses = [], []
    for window, dilation in A_PATTERNS:
        o, lse = dilated_pattern(q, k, v, rel_table, window, dilation)
        outs.append(o)
        lses.append(lse)
    w = jax.nn.softmax(jnp.stack(lses, axis=0), axis=0)
    return jnp.sum(w[..., None] * jnp.stack(outs, axis=0), axis=0)

def forgetting_attention(q, k, v, f_logit):
    B, S, H, Dh = q.shape
    c = jnp.cumsum(jax.nn.log_sigmoid(f_logit.astype(jnp.float32)), axis=1)
    cT = c.transpose(0, 2, 1)
    nq = S // BLOCK_Q
    qb = q.reshape(B, nq, BLOCK_Q, H, Dh).transpose(1, 0, 2, 3, 4)
    cb = cT.reshape(B, H, nq, BLOCK_Q).transpose(2, 0, 1, 3)
    kpos = jnp.arange(S)

    def block(args):
        n, qn, cn = args
        logits = jnp.einsum('bihd,bjhd->bhij', qn, k,
                            preferred_element_type=jnp.float32) * HEAD_DIM ** -0.5
        logits = logits + (cn[..., :, None] - cT[..., None, :])
        qpos = n * BLOCK_Q + jnp.arange(BLOCK_Q)
        logits = jnp.where(kpos[None, :] <= qpos[:, None], logits, -jnp.inf)
        p = jax.nn.softmax(logits, axis=-1)
        return jnp.einsum('bhij,bjhd->bihd', p.astype(v.dtype), v)

    ob = lax.map(block, (jnp.arange(nq), qb, cb))
    return ob.transpose(1, 0, 2, 3, 4).reshape(B, S, H, Dh)

def gla_chunked(q, k, v, log_alpha):
    B, S, H, DK = q.shape
    nc = S // C_CHUNK

    def chunks(t):
        return t.astype(jnp.float32).reshape(B, nc, C_CHUNK, H, t.shape[-1]).transpose(1, 0, 3, 2, 4)

    qc, kc, vc, gc = chunks(q * DK ** -0.5), chunks(k), chunks(v), chunks(log_alpha)
    causal = np.tril(np.ones((C_CHUNK, C_CHUNK), dtype=bool))[:, :, None]

    def step(state, inp):
        qn, kn, vn, gn = inp
        b = jnp.cumsum(gn, axis=2)
        o_inter = jnp.einsum('bhik,bhkv->bhiv', qn * jnp.exp(b), state)
        diff = b[:, :, :, None, :] - b[:, :, None, :, :]
        decay = jnp.exp(jnp.where(causal, diff, -jnp.inf))
        a = jnp.einsum('bhik,bhjk,bhijk->bhij', qn, kn, decay)
        o_intra = jnp.einsum('bhij,bhjv->bhiv', a, vn)
        b_last = b[:, :, -1:, :]
        state = state * jnp.exp(b_last[:, :, 0, :])[..., None] + \
            jnp.einsum('bhjk,bhjv->bhkv', kn * jnp.exp(b_last - b), vn)
        return state, o_inter + o_intra

    state0 = jnp.zeros((B, H, DK, v.shape[-1]), jnp.float32)
    _, o = lax.scan(step, state0, (qc, kc, vc, gc))
    return o.transpose(1, 0, 3, 2, 4).reshape(B, S, H, v.shape[-1])

def hybrid_mixer(h, w_in, f_bias, rel_table, c_gate_w2, c_gate_b, c_norm, w_out):
    B, S, _ = h.shape
    proj = h @ w_in
    qa, ka, va, qb, kb, vb, fl, qc, kc, vc, rc, gl = jnp.split(
        proj, np.cumsum(PROJ_SPLITS)[:-1].tolist(), axis=-1)

    def heads(t, n):
        return t.reshape(B, S, n, -1)

    o_a = dilated_mixture_attention(heads(qa, A_HEADS), heads(ka, A_HEADS), heads(va, A_HEADS), rel_table)
    o_b = forgetting_attention(heads(qb, B_HEADS), heads(kb, B_HEADS), heads(vb, B_HEADS), fl + f_bias)
    log_alpha = jax.nn.log_sigmoid((gl @ c_gate_w2 + c_gate_b).astype(jnp.float32)) / C_GATE_TAU
    o_c = gla_chunked(heads(qc, C_HEADS), heads(kc, C_HEADS), heads(vc, C_HEADS), heads(log_alpha, C_HEADS))
    o_c = rms_norm(o_c.astype(h.dtype), c_norm).reshape(B, S, C_VW) * jax.nn.silu(rc)
    mixed = jnp.concatenate([o_a.reshape(B, S, A_WIDTH).astype(h.dtype),
                             o_b.reshape(B, S, B_WIDTH).astype(h.dtype),
                             o_c.astype(h.dtype)], axis=-1)
    return mixed @ w_out

def memory_cross_attention(h, mem_n, w_q, w_kv, w_o):
    B, S, _ = h.shape
    M = mem_n.shape[1]
    q = (h @ w_q).reshape(B, S, CROSS_HEADS, CROSS_DH)
    k, v = jnp.split(mem_n @ w_kv, 2, axis=-1)
    k = k.reshape(B, M, CROSS_HEADS, CROSS_DH)
    v = v.reshape(B, M, CROSS_HEADS, CROSS_DH)
    logits = jnp.einsum('bshd,bmhd->bhsm', q, k, preferred_element_type=jnp.float32) * CROSS_DH ** -0.5
    p = jax.nn.softmax(logits, axis=-1)
    o = jnp.einsum('bhsm,bmhd->bshd', p.astype(v.dtype), v).reshape(B, S, CROSS_WIDTH)
    return o @ w_o

def conv_ffn(h, w_up, conv_w, conv_b, w_down):
    S = h.shape[1]
    val, gate = jnp.split(h @ w_up, 2, axis=-1)
    gp = jnp.pad(gate, ((0, 0), (CONV_W - 1, 0), (0, 0)))
    g = conv_b
    for i in range(CONV_W):
        g = g + conv_w[i] * gp[:, i:i + S]
    return (jax.nn.silu(g) * val) @ w_down

def second_inputs(seed: int = 0) -> dict:
    key = jax.random.key(seed)
    ks = jax.random.split(key, 21)

    def nrm(k, shape, scale):
        return jax.random.normal(k, shape, jnp.float32) * scale

    def gain(k, shape):
        return 1.0 + 0.05 * jax.random.normal(k, shape, jnp.float32)

    return {
        'x': nrm(ks[0], (BATCH, SEQ, D_MODEL), 1.0),
        'mem': nrm(ks[1], (BATCH, MEM_LEN, D_MODEL), 1.0),
        'rel_table': nrm(ks[2], (REL_BUCKETS, A_HEADS), 0.5),
        'mem_norm': gain(ks[3], (D_MODEL,)),
        'norm_final': gain(ks[4], (D_MODEL,)),
        'norm_mix': gain(ks[5], (DEPTH, D_MODEL)),
        'w_in': nrm(ks[6], (DEPTH, D_MODEL, PROJ_WIDTH), D_MODEL ** -0.5),
        'f_bias': 3.0 + nrm(ks[7], (DEPTH, B_HEADS), 0.1),
        'c_gate_w2': nrm(ks[8], (DEPTH, C_GATE_RANK, C_KW), C_GATE_RANK ** -0.5),
        'c_gate_b': nrm(ks[9], (DEPTH, C_KW), 0.1),
        'c_norm': gain(ks[10], (DEPTH, C_DV)),
        'w_out': nrm(ks[11], (DEPTH, MIX_WIDTH, D_MODEL), MIX_WIDTH ** -0.5),
        'norm_cross': gain(ks[12], (DEPTH, D_MODEL)),
        'w_cq': nrm(ks[13], (DEPTH, D_MODEL, CROSS_WIDTH), D_MODEL ** -0.5),
        'w_ckv': nrm(ks[14], (DEPTH, D_MODEL, 2 * CROSS_WIDTH), D_MODEL ** -0.5),
        'w_co': nrm(ks[15], (DEPTH, CROSS_WIDTH, D_MODEL), CROSS_WIDTH ** -0.5),
        'norm_ffn': gain(ks[16], (DEPTH, D_MODEL)),
        'w_up': nrm(ks[17], (DEPTH, D_MODEL, 2 * D_FF_2), D_MODEL ** -0.5),
        'conv_w': nrm(ks[18], (DEPTH, CONV_W, D_FF_2), CONV_W ** -0.5),
        'conv_b': nrm(ks[19], (DEPTH, D_FF_2), 0.02),
        'w_down': nrm(ks[20], (DEPTH, D_FF_2, D_MODEL), D_FF_2 ** -0.5),
    }

def second_block(x, mem, rel_table, mem_norm, norm_final, norm_mix, w_in, f_bias, c_gate_w2,
              c_gate_b, c_norm, w_out, norm_cross, w_cq, w_ckv, w_co, norm_ffn, w_up,
              conv_w, conv_b, w_down):
    mem_n = rms_norm(mem, mem_norm)
    for l in range(DEPTH):
        x = x + hybrid_mixer(rms_norm(x, norm_mix[l]), w_in[l], f_bias[l], rel_table,
                             c_gate_w2[l], c_gate_b[l], c_norm[l], w_out[l])
        x = x + memory_cross_attention(rms_norm(x, norm_cross[l]), mem_n, w_cq[l], w_ckv[l], w_co[l])
        x = x + conv_ffn(rms_norm(x, norm_ffn[l]), w_up[l], conv_w[l], conv_b[l], w_down[l])
    return rms_norm(x, norm_final)


def setup_inputs(seed=0):
    out = dict(first_inputs(seed))
    for name, value in second_inputs(seed + 1).items():
        if name != "x":
            out[name + "_2"] = value
    return out


def reference(
    x, c, w_ada, b_ada, pre_mix_norm, post_mix_norm, pre_ffn_norm, post_ffn_norm, w_in,
    hg_lb_logits, hg_norm, gdn_conv_w, gdn_a_log, gdn_dt_bias, gdn_norm, w_out, w_ff1, w_ff2,
    mem_2, rel_table_2, mem_norm_2, norm_final_2, norm_mix_2, w_in_2, f_bias_2, c_gate_w2_2,
    c_gate_b_2, c_norm_2, w_out_2, norm_cross_2, w_cq_2, w_ckv_2, w_co_2, norm_ffn_2, w_up_2,
    conv_w_2, conv_b_2, w_down_2,
):
    x = first_block(
        x, c, w_ada, b_ada, pre_mix_norm, post_mix_norm, pre_ffn_norm, post_ffn_norm, w_in,
        hg_lb_logits, hg_norm, gdn_conv_w, gdn_a_log, gdn_dt_bias, gdn_norm, w_out, w_ff1,
        w_ff2,
    )
    return second_block(
        x, mem_2, rel_table_2, mem_norm_2, norm_final_2, norm_mix_2, w_in_2, f_bias_2,
        c_gate_w2_2, c_gate_b_2, c_norm_2, w_out_2, norm_cross_2, w_cq_2, w_ckv_2, w_co_2,
        norm_ffn_2, w_up_2, conv_w_2, conv_b_2, w_down_2,
    )


_drawn_inputs = setup_inputs


def setup_inputs(seed=0):
    import zlib

    import numpy as np

    out = dict(_drawn_inputs(seed))
    spreads = {}
    factors = {'post_mix_norm': 2.737,
     'pre_ffn_norm': 2.821,
     'post_ffn_norm': 2.968,
     'hg_norm': 3.543,
     'gdn_norm': 4.416,
     'mem_norm_2': 7.797,
     'f_bias_2': 64.0,
     'c_gate_b_2': 4.271,
     'c_norm_2': 3.324,
     'norm_cross_2': 8.0,
     'conv_b_2': 36.177,
     'norm_ffn_2': 8.0}
    for name, (base, spread) in spreads.items():
        noise = np.random.default_rng([zlib.crc32(name.encode()), seed]).standard_normal(out[name].shape)
        drawn = base * np.exp(spread * noise) if base else spread * noise
        out[name] = __import__('jax').numpy.asarray(drawn.astype(out[name].dtype))
    for name, factor in factors.items():
        out[name] = (out[name] * factor).astype(out[name].dtype)
    return out
```

```python
import numpy as np
import concourse.bass as bass
from concourse import mybir
from contextlib import ExitStack

F32 = mybir.dt.float32
F32R = mybir.dt.float32r
U8 = mybir.dt.uint8
ALU = mybir.AluOpType
ACT = mybir.ActivationFunctionType
AX = mybir.AxisListType.X
ds = bass.ds

D, T = 2048, 256
KT = D // 128
TT = T // 128
CH = 64
H1, DH = 8, 128
GRP = H1 * DH
INC = 8 * GRP + 2 * H1
DFF = 4 * D
EPS = 1e-6
AH, BH, HD = 12, 8, 64
CH2, CK, CV = 4, 96, 192
INC2 = 3 * AH * HD + 3 * BH * HD + BH + 2 * CH2 * CK + 2 * CH2 * CV + 16
XH, XD = 4, 128
DFF2 = 5504
UW = 1024
RAWN, SPN = 4, 4
LEVELS = (1, 2, 4, 8, 16, 32)
FAR = -1.0e30


class Chunk:

    def __init__(self, w, row0, col0, kn, width, lhs, out, row_step=0, col_step=0, ada=None, phase=None, mid=0):
        self.w, self.row0, self.col0, self.kn, self.width = w, row0, col0, kn, width
        self.lhs, self.out, self.row_step, self.col_step = lhs, out, row_step, col_step
        self.ada, self.phase, self.mid = ada, phase, mid
        self.banks = TT * (-(-width // 512))

    def ada_after(self, j):
        return self.mid * (j == 1) if self.mid else int(bool(self.ada) and j % 2 == 1)

    def load_of(self, j):
        return self.at["n"] + j + sum(self.ada_after(x) for x in range(j))


def number(segments, first_dma):
    u, n, done, signals, prev = 0, first_dma, [0] * 4, [0] * 4, None
    rel = {m: ("ada", m + 1) for m in range(first_dma)}
    ada = first_dma
    for iters, chunks in segments:
        for i in range(iters):
            for c in chunks:
                now = dict(u=u, n=n, ada=ada, done=list(done), signals=list(signals), prev=(prev or {}).get("end"))
                for k in range(0, c.kn, 2):
                    u += min(2, c.kn - k)
                    rel[n] = ("lo", u)
                    n += 1
                    for _ in range(c.ada_after(k // 2)):
                        ada += 1 if c.mid else 2
                        rel[n] = ("ada", ada)
                        n += 1
                for b in range(c.banks):
                    done[b] += 1
                    signals[b] += b < c.banks - 1
                now["end"] = dict(u=u, done=list(done), banks=c.banks, width=c.width, out=c.out,
                                  col=c.out[2] + i * c.out[3])
                if i == 0:
                    c.at = now
                elif i == 1:
                    c.step = now
                prev = now
    for iters, chunks in segments:
        for c in chunks:
            a, b = c.at, (c.step if iters > 1 else c.at)
            c.du, c.dn, c.dada = b["u"] - a["u"], b["n"] - a["n"], b["ada"] - a["ada"]
            c.ddone = [y - x for x, y in zip(a["done"], b["done"])]
            assert c.du % SPN == 0 and c.dn % RAWN == 0
            if iters > 1:
                for m in range(a["n"], c.load_of(-(-c.kn // 2))):
                    if m >= RAWN:
                        x, y = rel[m - RAWN], rel[m + c.dn - RAWN]
                        assert x[0] == y[0] and y[1] - x[1] == (c.du if x[0] == "lo" else c.dada)
    tail = Chunk(None, 0, 0, 0, 0, None, None)
    tail.at = dict(u=u, n=n, ada=ada, done=list(done), signals=list(signals), prev=prev["end"])
    tail.du = tail.dn = tail.dada = 0
    tail.ddone = [0] * 4
    return rel, tail


def val(base, step, i):
    return base if i is None else i * step + base


def shape_constants():
    a, b = np.arange(128)[:, None], np.arange(128)[None, :]
    same = a // CH == b // CH
    f = np.stack([a == b, a >= 0 * b, same & (a <= b), same & (a > b), a <= b], 1).astype(np.float32)
    neg = np.where(b <= a, 0.0, FAR).astype(np.float32)
    f = np.concatenate([f, neg[:, None]], 1)
    lv = [(a // (2 * m) == b // (2 * m)) & (a % (2 * m) < m) & (b % (2 * m) >= m) for m in LEVELS]
    u = np.stack([a == b] + lv + [lv[0].T], 1).astype(np.float32)
    d = 255 - np.arange(384)
    e = np.maximum(d, 1).astype(np.float32)
    large = 16 + (np.log(e / 16) / np.log(2048 / 16) * 16).astype(np.int32)
    bucket = np.where(d < 16, d, np.minimum(large, 31))
    count = (d <= 128).astype(int) + (d % 4 == 0) + (d % 16 == 0)
    oh = np.zeros((33, 384), np.float32)
    for j in range(384):
        if d[j] >= 0 and count[j] > 0:
            oh[bucket[j], j] = 1.0
            oh[32, j] = np.log(count[j])
        else:
            oh[32, j] = FAR
    return f.reshape(128, -1), u.reshape(128, -1), oh


def block_pair(nc, a, out, stop=None):
    with ExitStack() as ctx:
        sems = {}

        def S(name):
            if name not in sems:
                sems[name] = ctx.enter_context(nc.semaphore(name))
            return sems[name]

        def psb(name, shape, dt=F32):
            return ctx.enter_context(nc.sbuf_tensor(name, shape, dt))

        def region(*parts):
            with ExitStack() as r:
                return [r.enter_context(nc.sbuf_tensor(*p)) for p in parts]

        RAW = psb("raw_weights", [128, RAWN, 2, UW])
        WHI = psb("weights_high", [128, SPN, UW], F32R)
        WLO = psb("weights_low", [128, SPN, UW], F32R)
        MOD = psb("modulation", [128, 4, D])
        CF = psb("tables", [128, 6, 128])
        CM = psb("masks", [128, 8, 128], U8)
        COLS = psb("columns", [128, 384])
        ROWS = psb("small_rows", [128, 496])
        GATES = psb("gates", [128, 10, 16])
        SM = psb("small", [128, 256])
        IDENT, ONES, UPPER, AFTER, UPPER_ALL, CAUSAL = (CF[:, j, :] for j in range(6))
        LT = [("lhs_high", [128, KT, T], F32R), ("lhs_low", [128, KT, T], F32R)]
        LH, LL, P = region(*LT, ("proj", [128, TT, INC], F32))
        _, _, XN, HN, VEC0, MODA, TOE, REL = region(*[(f"n1_{n}", s, d) for n, s, d in LT], ("x_rows", [128, TT, D], F32),
                                          ("h_rows", [128, TT, D], F32), ("vec0", [128, D], F32),
                                          ("mod_in", [128, 2, D], F32), ("distance_rows", [128, 4, 384], F32),
                                          ("relative", [33, AH + 384], F32))
        (LB,) = region(("scratch", [128, 4, TT * GRP], F32))
        LH2, LL2, X, Y, L2H, L2L, NAT, VEC = region(
            ("lhs2_high", [128, KT, T], F32R), ("lhs2_low", [128, KT, T], F32R),
            ("x2_rows", [128, TT, D], F32), ("y_rows", [128, TT, D], F32),
            ("hid_high", [128, 8, T], F32R), ("hid_low", [128, 8, T], F32R), ("hid_rows", [128, TT, UW], F32),
            ("vec", [128, D], F32))
        _, _, _, P2 = region(("q0", [128, KT, T], F32R), ("q1", [128, KT, T], F32R), ("q2", [128, TT, D], F32),
                             ("proj2", [128, TT, INC2], F32))
        PS = ctx.enter_context(nc.psum_tensor("banks", [128, 8, 512], F32))

        def ck(name, row0, col0, kn, width, lhs, outp, **kw):
            return Chunk(a[name], row0, col0, kn, width, lhs, outp, **kw)

        first = (LH, LL)
        second = (LH2, LL2)
        hid = (L2H, L2L)

        def whole(name, out_kind, tensor, cols, lhs=second, kn=KT, hooks0=None):
            chunks = []
            for c0 in range(0, cols, UW):
                w = min(UW, cols - c0)
                chunks.append(ck(name, 0, c0, kn, w, lhs, (out_kind, tensor, c0, 0), phase=hooks0 if c0 == 0 else None))
            return chunks

        def pair_in(base, step, iters, half_row, phases=(None, None)):
            return (iters, [ck("w_in", 0, (base + j) * UW, KT, UW, first, ("copy", P, (base + j) * UW, step * UW),
                               col_step=step * UW, ada=(half_row, 1, 4 * j), phase=phases[j]) for j in range(2)])

        def up1(c, step=0, phase=None, ada=None):
            return ck("w_ff1", 0, c * UW, KT, UW, second, ("relu", NAT, 0, 0), col_step=step * UW, phase=phase, ada=ada)

        def down1(c, step=0, phase=None, ada=(None, None)):
            return [ck("w_ff2", c * UW, h * UW, 8, UW, hid, ("add", Y, h * UW, 0), row_step=step * UW,
                       phase=phase if h == 0 else "none", ada=ada[h]) for h in range(2)]

        MODF = MOD[:, :, :].rearrange("p c d -> p (c d)")
        NATG, NATV = MOD[:, 0, :].rearrange("p (t n) -> p t n", t=TT), MOD[:, 1, :].rearrange("p (t n) -> p t n", t=TT)

        def up2(c, step=0, phases=(None, None)):
            w = min(UW, DFF2 - c * UW)
            return [ck("w_up_2", 0, (1 - g) * DFF2 + c * UW, KT, w, second, ("copy", (NATG, NATV)[g], 0, 0),
                       col_step=step * UW, phase=phases[g]) for g in range(2)]

        def down2(c, step=0, phase=None):
            kn = min(8, (DFF2 - c * UW) // 128)
            return [ck("w_down_2", c * UW, h * UW, kn, UW, hid, ("add", X, h * UW, 0), row_step=step * UW,
                       phase=phase if h == 0 else "none") for h in range(2)]

        KV = MOD[:, 2, :].rearrange("p (t n) -> p t n", t=TT)
        QX = MOD[:, 3, 0:1024].rearrange("p (t n) -> p t n", t=TT)
        segs = [(1, [ck("w_in", 0, 8 * UW, KT, INC - 8 * UW, first, ("copy", P, 8 * UW, 0), phase="norm_in")]),
                pair_in(4, 0, 1, 0, (None, "conv0")), pair_in(6, 0, 1, 1, ("conv1", "conv2")), pair_in(0, 2, 2, 2)]
        in_segs = len(segs)
        stages = {
            "mix1": [(1, whole("w_out", "copy", Y, D, hooks0="mix1"))],
            "ffn1": [(1, [up1(0, phase="norm_ffn1", ada=(6, 0, 4))]), (1, [up1(1, phase="hid1")]),
                     (6, down1(0, 1, "hid_wait") + [up1(2, 1, "hid1")]),
                     (1, down1(6, phase="hid_wait", ada=((7, 0, 0), (7, 0, 2)))),
                     (1, down1(7, phase="hid1_last", ada=((7, 0, 4), (7, 0, 6))))],
            "in2": [(1, whole("w_in_2", "copy", P2, INC2, hooks0="norm_in2"))],
            "mix2": [(1, whole("w_out_2", "add", X, D, hooks0="mix2"))],
            "kv": [(1, whole("w_ckv_2", "copy", KV, 2 * XH * XD, hooks0="norm_mem"))],
            "cq": [(1, whole("w_cq_2", "copy", QX, XH * XD, hooks0="norm_cross"))],
            "co": [(1, whole("w_co_2", "add", X, D, kn=4, hooks0="cross"))],
            "ffn2": [(1, up2(0, phases=("norm_ffn2", None))), (1, up2(1, phases=("hid2", None))),
                     (4, down2(0, 1, "hid_wait") + up2(2, 1, ("hid2", None))),
                     ],
        }
        stages["ffn2"][2] = (3, down2(0, 1, "hid_wait") + up2(2, 1, ("hid2", None)))
        stages["ffn2"] += [(1, down2(3, phase="hid_wait") + up2(5, 0, ("hid2", None))),
                           (1, down2(4, phase="hid_wait")), (1, down2(5, phase="hid2_last"))]
        for name, part in stages.items():
            if stop == "in" :
                break
            segs += part
            if name == {"mx": "mix2"}.get(stop, stop):
                break
        if stop != "in":
            segs[in_segs][1][0].mid = KT
            segs[in_segs][1][1].ada = (6, 0, 0)
        first_dma = 2 * KT
        RELEASE, TAIL = number(segs, first_dma)

        round_of, r = {}, 0
        for nm, k in (("norm_in", 8), ("conv", 12), ("mix1", 8), ("norm_ffn1", 8), ("hid1", 28), ("hid1_last", 4), ("norm_in2", 8),
                      ("mix2", 8), ("norm_mem", 8), ("norm_cross", 8), ("cross", 2), ("norm_ffn2", 8),
                      ("hid2", 64)):
            round_of[nm] = r
            r += k

        def sp_chunk(sp, c, i):
            n = c.at["n"]

            def load(dst, src):
                nonlocal n
                if n >= RAWN:
                    kind, value = RELEASE[n - RAWN]
                    sp.wait_ge(S("low_made" if kind == "lo" else "ada_used"),
                               val(value, c.du if kind == "lo" else c.dada, i))
                sp.dma_start(dst, src).then_inc(S(f"weights_in{n % RAWN}"), 16)
                n += 1

            for k in range(0, c.kn, 2):
                m = min(2, c.kn - k)
                r0, c0 = val(c.row0 + k * 128, c.row_step, i), val(c.col0, c.col_step, i)
                rows = slice(r0, r0 + m * 128) if isinstance(r0, int) else ds(r0, m * 128)
                cols = slice(c0, c0 + c.width) if isinstance(c0, int) else ds(c0, c.width)
                load(RAW[:, n % RAWN, 0:m, 0:c.width], c.w[rows, cols].rearrange("(j p) n -> p j n", p=128))
                for x in range(c.ada_after(k // 2)):
                    if c.mid:
                        load(RAW[:, n % RAWN, :, :].rearrange("p j n -> p (j n)"),
                             a["w_ada"][x * 128:x * 128 + 128, 4 * D:5 * D])
                        continue
                    half_row, step, pair = c.ada
                    x0, q = val(2 * D + half_row * UW, step * UW, i), pair + k // 4
                    xs = slice(x0, x0 + UW) if isinstance(x0, int) else ds(x0, UW)
                    load(RAW[:, n % RAWN, :, :], a["w_ada"][q * 256:q * 256 + 256, xs].rearrange("(j p) n -> p j n", p=128))

        def sp_ada_first(sp):
            for n in range(2 * KT):
                comp, kt = divmod(n, KT)
                if n >= RAWN:
                    sp.wait_ge(S("ada_used"), n - RAWN + 1)
                sp.dma_start(RAW[:, n % RAWN, :, :].rearrange("p j n -> p (j n)"),
                             a["w_ada"][kt * 128:kt * 128 + 128, comp * D:comp * D + D]).then_inc(
                                 S(f"weights_in{n % RAWN}"), 16)

        def unit_dma(c, k):
            return c.load_of(k // 2)

        def act_chunk(act, c, i, hooks, evac):
            for k in range(c.kn):
                u, n = c.at["u"] + k, unit_dma(c, k)
                act.wait_ge(S(f"weights_in{n % RAWN}"), val(16 * (n // RAWN + 1), 16 * (c.dn // RAWN), i))
                if u >= SPN:
                    act.wait_ge(S("unit_used"), val(u - SPN + 1, c.du, i))
                act.activation(WHI[:, u % SPN, 0:c.width], RAW[:, n % RAWN, k % 2, 0:c.width],
                               ACT.Copy).then_inc(S("high_made"), 1)
                if k == 2:
                    evac(act, c, i)
                if k >= 2:
                    hooks(c, k - 2, i)

        def dve_chunk(dve, c, i, hooks, evac):
            for k in range(c.kn):
                u, n = c.at["u"] + k, unit_dma(c, k)
                dve.wait_ge(S("high_made"), val(u + 1, c.du, i))
                dve.tensor_tensor(WLO[:, u % SPN, 0:c.width], RAW[:, n % RAWN, k % 2, 0:c.width],
                                  WHI[:, u % SPN, 0:c.width].bitcast(F32), ALU.subtract).then_inc(S("low_made"), 1)
                if c.ada and k % 4 == 3:
                    half_row, step, pair = c.ada
                    m0 = val(half_row * UW, step * UW, i)
                    acc = MODF[:, slice(m0, m0 + UW) if isinstance(m0, int) else ds(m0, UW)]
                    m = n + 1
                    dve.wait_ge(S(f"weights_in{m % RAWN}"), val(16 * (m // RAWN + 1), 16 * (c.dn // RAWN), i))
                    for j in range(2):
                        ada_step(dve, acc, RAW[:, m % RAWN, j, :], 2 * (pair + k // 4) + j,
                                 val(c.at["ada"] + 2 * (k // 4) + j, c.dada, i))
                if k == 2:
                    evac(dve, c, i)
                if k >= 2:
                    hooks(c, k - 2, i)

        def ada_step(dve, acc, row, kt, done):
            if done is not None:
                dve.wait_ge(S("ada_used"), done)
            dve.scalar_tensor_tensor(out=acc, in0=row, scalar=COLS[:, 112 + kt:113 + kt], in1=acc,
                                     op0=ALU.mult, op1=ALU.add).then_inc(S("ada_used"), 1)

        def pe_chunk(pe, c, i, hooks):
            lh, ll = c.lhs
            halves = [(h, min(512, c.width - 512 * h)) for h in range(-(-c.width // 512))]
            for k in range(c.kn):
                hooks(c, k, i)
                u = c.at["u"] + k
                pe.wait_ge(S("low_made"), val(u + 1, c.du, i))
                s = u % SPN
                for h, w in halves:
                    hi, lo = WHI[:, s, 512 * h:512 * h + w], WLO[:, s, 512 * h:512 * h + w]
                    for t in range(TT):
                        b = 2 * h + t
                        if k == 0 and c.at["done"][b] > 0:
                            pe.wait_ge(S(f"bank_free{b}"), val(c.at["done"][b], c.ddone[b], i))
                        tk = slice(128 * t, 128 * t + 128)
                        o = PS[:, b, 0:w]
                        nc.tensor.matmul(o, lh[:, k, tk], hi, start=(k == 0), stop=False)
                        nc.tensor.matmul(o, lh[:, k, tk], lo, start=False, stop=False)
                        mm = nc.tensor.matmul(o, ll[:, k, tk], hi, start=False, stop=(k == c.kn - 1))
                        if b == c.banks - 1:
                            mm.then_inc(S("unit_used"), 1)
                        elif k == c.kn - 1:
                            mm.then_inc(S(f"bank_done{b}"), 1)

        def out_banks(c, i, kinds):
            p = c.at["prev"]
            if p is None or p["out"][0] not in kinds:
                return
            q = c.step["prev"] if i is not None else p
            for b in range(p["banks"]):
                h, t = divmod(b, 2)
                count = val(p["done"][b], c.ddone[b], i)
                unit = val(p["u"], c.du, i)
                last = b == p["banks"] - 1
                yield (b, t, h, min(512, p["width"] - 512 * h), count, (S("unit_used"), unit) if last else
                       (S(f"bank_done{b}"), DONE_BUT_LAST(c, b, i)), val(p["col"], q["col"] - p["col"], i))

        def DONE_BUT_LAST(c, b, i):
            base, step = c.at["signals"][b], c.step["signals"][b] - c.at["signals"][b] if i is not None else 0
            return val(base, step, i)

        def act_evac(act, c, i):
            for b, t, h, w, count, (sem, value), col in out_banks(c, i, ("copy", "relu")):
                kind, dst = c.at["prev"]["out"][0:2]
                act.wait_ge(sem, value)
                lo = col + 512 * h
                o = dst[:, t, lo:lo + w] if isinstance(lo, int) else dst[:, t, ds(lo, w)]
                act.activation(o, PS[:, b, 0:w], ACT.Relu if kind == "relu" else ACT.Copy).then_inc(
                    S(f"bank_free{b}"), 1)

        def dve_evac(dve, c, i):
            for b, t, h, w, count, (sem, value), col in out_banks(c, i, ("add",)):
                dve.wait_ge(sem, value)
                o = c.at["prev"]["out"][1][:, t, col + 512 * h:col + 512 * h + w]
                dve.tensor_tensor(o, o, PS[:, b, 0:w], ALU.add).then_inc(S(f"bank_free{b}"), 1)
            for b, t, h, w, count, _, _ in out_banks(c, i, ("relu",)):
                dve.wait_ge(S(f"bank_free{b}"), count)
                o = NAT[:, t, 512 * h:512 * h + w]
                dve.tensor_tensor(o, o, o, ALU.mult).then_inc(S("hid_squared"), 1)

        def pe_round(pe, r, rows, kt0, nk, i=None, step=0, f0=0):
            if r >= 4:
                pe.wait_ge(S("round_free"), val(r - 3, step, i))
            bank = PS[:, 4 + r % 4, :].rearrange("p (k t) -> p k t", k=2)
            for k in range(nk):
                for t in range(TT):
                    c0 = f0 + (kt0 + k) * 128
                    tr = nc.tensor.transpose(bank[:, k, 128 * t:128 * t + 128], rows[:, t, c0:c0 + 128], IDENT)
            tr.then_inc(S("round_ready"), 1)

        def act_round(act, r, lh, kt0, nk, i=None, step=0):
            act.wait_ge(S("round_ready"), val(r + 1, step, i))
            act.activation(lh[:, kt0:kt0 + nk, :].rearrange("p k t -> p (k t)"), PS[:, 4 + r % 4, 0:nk * T],
                           ACT.Copy).then_inc(S("round_high"), 1)

        HIGHS = {}

        def dve_round(dve, r, lh, ll, kt0, nk, nhigh, i=None, step=0, hstep=0):
            dve.wait_ge(S("round_high"), val(nhigh, hstep, i))
            dve.tensor_tensor(ll[:, kt0:kt0 + nk, :].rearrange("p k t -> p (k t)"), PS[:, 4 + r % 4, 0:nk * T],
                              lh[:, kt0:kt0 + nk, :].rearrange("p k t -> p (k t)").bitcast(F32),
                              ALU.subtract).then_inc(S("round_free"), 1)

        nhigh_of = {nm: r - (0 if nm == "norm_in" else 12) for nm, r in round_of.items()}

        def pe_split(pe, name, rows, nk=KT, ready=None):
            halves = ready and ready[0] is S("h_ready") and ready[1] > 1
            if ready:
                pe.wait_ge(ready[0], ready[1] - 1 if halves else ready[1])
            r0 = round_of[name]
            for j in range(0, nk, 2):
                if halves and j == nk // 2:
                    pe.wait_ge(*ready)
                pe_round(pe, r0 + j // 2, rows, j, min(2, nk - j))
            pe.wait_ge(S("round_free"), r0 + (nk + 1) // 2)

        def act_split(act, name, lh, nk=KT):
            for j in range(0, nk, 2):
                act_round(act, round_of[name] + j // 2, lh, j, min(2, nk - j))

        def dve_split(dve, name, lh, ll, nk=KT):
            for j in range(0, nk, 2):
                dve_round(dve, round_of[name] + j // 2, lh, ll, j, min(2, nk - j), nhigh_of[name] + j // 2 + 1)

        class Chain:
            n = 0

            def __init__(self, eng):
                self.eng = eng

            def __call__(self, ins):
                Chain.n += 1
                ins.then_inc(S("vector_step"), 1)
                self.eng.wait_ge(S("vector_step"), Chain.n)

        NORMS = ["norm_in", "hg_heads", "gdn_heads", "post_mix", "pre_ffn", "post_ffn", "mix_in", "gla_heads", "mem",
                 "cross_in", "ffn2_in", "final"]

        def act_squares(act, name, rows, n=D):
            m, q = NORMS.index(name), NSQ.index(name)
            for t in range(TT):
                act.wait_ge(S("rows_ready"), 2 * q - 1 + t)
                sq = act.activation(PS[:, 4:8, :].rearrange("p b n -> p (b n)"), rows[:, t, :], ACT.Square,
                                    accum_out=SM[:, 2 * m + t:2 * m + t + 1])
                sq.then_inc(S("squares_summed"), 1)
                act.wait_ge(S("squares_summed"), 2 * q + t + 1)

        NSQ = [n for n in NORMS if not n.endswith("heads")]

        def rstd(name, t):
            m = NORMS.index(name)
            return SM[:, 2 * m + t:2 * m + t + 1]

        MEANS_BEFORE = {n: sum(1 if x.endswith("heads") else TT for x in NORMS[:m]) for m, n in enumerate(NORMS)}

        def dve_rstd(dve, name, t=None, stat=None, n=D):
            if stat is None:
                dve.wait_ge(S("squares_summed"), 2 * NSQ.index(name) + t + 1)
                stat = rstd(name, t)
            dve.tensor_scalar(stat, stat, 1.0 / n, EPS, ALU.mult, ALU.add).then_inc(S("mean_ready"), 1)
            dve.wait_ge(S("rstd_ready"), MEANS_BEFORE[name] + (t or 0) + 1)

        def pool_rstd(pool, name, stat=None):
            for t, x in enumerate([rstd(name, t) for t in range(TT)] if stat is None else [stat]):
                pool.wait_ge(S("mean_ready"), MEANS_BEFORE[name] + t + 1)
                nc.gpsimd.tensor_tensor(x, x, MINUS_HALF[:, 0:x.shape[1]], ALU.pow).then_inc(S("rstd_ready"), 1)

        MINUS_HALF = SM[:, 240:256]

        def row_vector(name, cols=D):
            return a[name].rearrange("(o n) -> o n", o=1).to_broadcast([128, cols])

        STG = HN[:, 0, 0:384].rearrange("p (s n) -> p s n", s=3)

        def pool_start(pool):
            pool.dma_start(CF[:, :, :].rearrange("p j n -> p (j n)"), a["table_f"]).then_inc(S("tables_in"), 16)
            pool.dma_start(HN[:, 1, 0:1024], a["table_m"]).then_inc(S("tables_in"), 16)
            pool.memset(MINUS_HALF, -0.5).then_inc(S("half_set"), 1)
            pool.wait_ge(S("half_set"), 1)
            pool.wait_ge(S("cleared"), 1)
            for dst, src in (
                    (STG[0:96, 0, :], a["gdn_conv_w"].rearrange("j (b p) -> (j b) p", p=128)),
                    (STG[96:112, 0, :], a["hg_lb_logits"].rearrange("l h k -> (l h) k")),
                    (STG[112:128, 0, :], a["c"].rearrange("o (k p) -> (o k) p", p=128)),
                    (STG[0:86, 1, :], a["conv_w_2"][0:2, :].rearrange("j (b p) -> (j b) p", p=128)),
                    (STG[86:90, 1, 0:CK], a["c_gate_b_2"].rearrange("(h k) -> h k", k=CK)),
                    (STG[0:43, 2, :], a["conv_w_2"][2:3, :].rearrange("j (b p) -> (j b) p", p=128)),
                    (STG[43:86, 2, :], a["conv_b_2"].rearrange("(b p) -> b p", p=128))):
                pool.dma_start(dst, src).then_inc(S("columns_in"), 16)
            pool.dma_start(MODA[0:1, :, :].rearrange("o c d -> o (c d)"),
                           a["b_ada"][0:2 * D].rearrange("(o n) -> o n", o=1)).then_inc(S("bias_in"), 16)
            pool.dma_start(MOD[0:1, :, :].rearrange("o c d -> o (c d)"),
                           a["b_ada"][2 * D:6 * D].rearrange("(o n) -> o n", o=1)).then_inc(S("bias_in"), 16)
            pool.dma_start(XN[:, :, :], a["x"].rearrange("(t p) d -> p t d", p=128)).then_inc(S("x_in"), 16)
            pool.dma_start(VEC0[:, :], row_vector("pre_mix_norm")).then_inc(S("vec0_in"), 16)
            for k0, name, n in ROW_VECTORS:
                pool.dma_start(ROWS[:, k0:k0 + n], row_vector(name, n)).then_inc(S("rows_in"), 16)
            pool.memset(REL[32:33, 0:AH], 1.0).then_inc(S("rel_one"), 1)
            pool.dma_start(REL[0:32, 0:AH], a["rel_table_2"]).then_inc(S("rel_in"), 16)
            pool.dma_start(REL[0:33, AH:AH + 384], a["distances"]).then_inc(S("rel_in"), 16)
            for h in range(AH):
                pool.wait_ge(S("distance_row"), h + 1)
                pool.dma_start(a["toeplitz"][h, :, :], TOE[:, h % 4, :]).then_inc(S(f"table_out{h % 4}"), 16)
            pool_rstd(pool, "norm_in")

        ROW_VECTORS = [(0, "hg_norm", 128), (128, "gdn_norm", 128), (256, "gdn_a_log", 8), (264, "gdn_dt_bias", 8),
                       (272, "f_bias_2", 8), (296, "c_norm_2", CV)]

        def dve_start(dve):
            link = Chain(dve)
            dve.memset(STG, 0.0)
            dve.memset(MODA[:, :, :], 0.0)
            dve.memset(MOD[:, :, :], 0.0).then_inc(S("cleared"), 1)
            dve.wait_ge(S("tables_in"), 32)
            link(dve.tensor_copy(CM[:, :, :].rearrange("p j n -> p (j n)"), HN[:, 1, 0:1024]))
            dve.wait_ge(S("columns_ready"), 3)
            for s, rows in enumerate((128, 90, 86)):
                last = dve.tensor_copy(COLS[:, 128 * s:128 * s + rows], PS[:, s, 0:rows])
            link(last)
            cc, l0, l1, tmp = COLS[:, 112:128], COLS[:, 96:104], COLS[:, 104:112], SM[:, 200:216]
            link(dve.tensor_tensor(tmp[:, 0:8], l0, l1, ALU.max))
            link(dve.tensor_tensor(l0, l0, tmp[:, 0:8], ALU.subtract))
            dve.tensor_tensor(l1, l1, tmp[:, 0:8], ALU.subtract).then_inc(S("logits_shifted"), 1)
            dve.wait_ge(S("start_exp"), 2)
            link(dve.tensor_tensor(tmp[:, 0:8], l0, l1, ALU.add))
            link(dve.reciprocal(tmp[:, 0:8], tmp[:, 0:8]))
            link(dve.tensor_tensor(l0, l0, tmp[:, 0:8], ALU.mult))
            link(dve.tensor_scalar(l1, l0, -1.0, 1.0, ALU.mult, ALU.add))
            link(dve.tensor_scalar(SM[:, 216:232], SM[:, 216:232], 1.0, None, ALU.add))
            link(dve.reciprocal(SM[:, 216:232], SM[:, 216:232]))
            link(dve.tensor_tensor(cc, cc, SM[:, 216:232], ALU.mult))
            dve.wait_ge(S("bias_in"), 32)
            for n in range(2 * KT):
                comp, kt = divmod(n, KT)
                dve.wait_ge(S(f"weights_in{n % RAWN}"), 16 * (n // RAWN + 1))
                ada_step(dve, MODA[:, comp, :], RAW[:, n % RAWN, :, :].rearrange("p j n -> p (j n)"), kt, n if kt else None)

        def act_start(act):
            act.wait_ge(S("logits_shifted"), 1)
            act.activation(COLS[:, 96:112], COLS[:, 96:112], ACT.Exp).then_inc(S("start_exp"), 1)
            act.activation(SM[:, 216:232], COLS[:, 112:128], ACT.Exp, scale=-1.0).then_inc(S("start_exp"), 1)

            for h in range(AH):
                act.wait_ge(S("distances_ready"), h + 1)
                if h >= 4:
                    act.wait_ge(S(f"table_out{h % 4}"), 16 * (h // 4))
                act.activation(TOE[:, h % 4, :], PS[:, 4 + h % 4, 0:384], ACT.Copy).then_inc(S("distance_row"), 1)

        def pe_start(pe):
            pe.wait_ge(S("tables_in"), 32)
            pe.wait_ge(S("columns_in"), 7 * 16)
            for s, rows in enumerate((128, 90, 86)):
                nc.tensor.transpose(PS[:, s, 0:rows], STG[0:rows, s, :], CF[0:rows, 0, 0:rows]).then_inc(
                    S("columns_ready"), 1)

            pe.wait_ge(S("rel_in"), 32)
            pe.wait_ge(S("rel_one"), 1)
            for h in range(AH):
                if h >= 4:
                    pe.wait_ge(S("distance_row"), h - 3)
                nc.tensor.matmul(PS[:, 4 + h % 4, 0:384], REL[0:33, h:h + 1].to_broadcast([33, 128]),
                                 REL[0:33, AH:AH + 384], start=True, stop=True).then_inc(S("distances_ready"), 1)

        def pe_norm_in(pe):
            pe.wait_ge(S("ada_used"), 2 * KT)
            pe.wait_ge(S("distance_row"), AH)
            for b in range(8):
                comp, q = divmod(b, 4)
                nc.tensor.matmul(PS[:, b, :], ONES, MODA[:, comp, 512 * q:512 * q + 512], start=True,
                                 stop=True).then_inc(S("mod_in_ready"), 1)
            pe_split(pe, "norm_in", HN, ready=(S("h_ready"), 1))

        def act_norm_in(act):
            act.wait_ge(S("x_in"), 16)
            for t in range(TT):
                act.activation(HN[:, t, :], XN[:, t, :], ACT.Square, accum_out=SM[:, t:t + 1]).then_inc(
                    S("squares_summed"), 1)
            act.wait_ge(S("mod_in_ready"), 4)
            act.activation(MODA[:, 0, :], PS[:, 0:4, :].rearrange("p b n -> p (b n)"), ACT.Copy).then_inc(
                S("shift_in"), 1)
            for j in range(4):
                act.wait_ge(S(f"table_out{j}"), 16 * (AH // 4))
            act_split(act, "norm_in", LH)

        def dve_norm_in(dve):
            link = Chain(dve)
            dve.wait_ge(S("vec0_in"), 16)
            dve.wait_ge(S("mod_in_ready"), 8)
            link(dve.scalar_tensor_tensor(out=MODA[:, 1, :], in0=PS[:, 4:8, :].rearrange("p b n -> p (b n)"), scalar=1.0,
                                          in1=VEC0[:, :], op0=ALU.add, op1=ALU.mult))
            for t in range(TT):
                dve_rstd(dve, "norm_in", t)
                link(dve.scalar_tensor_tensor(out=HN[:, t, :], in0=XN[:, t, :], scalar=rstd("norm_in", t),
                                              in1=MODA[:, 1, :], op0=ALU.mult, op1=ALU.mult))
            dve.wait_ge(S("shift_in"), 1)
            link(dve.tensor_tensor(HN[:, 0, :], HN[:, 0, :], MODA[:, 0, :], ALU.add))
            dve.tensor_tensor(HN[:, 1, :], HN[:, 1, :], MODA[:, 0, :], ALU.add).then_inc(S("h_ready"), 1)
            dve_split(dve, "norm_in", LH, LL)

        class Decay:
            def __init__(self, first, H, dk, dv, qT, kT, bT, qm, km, at, kn, v, st, tails):
                self.first, self.H, self.dk, self.dv = first, H, dk, dv
                self.qT, self.kT, self.bT, self.qm, self.km, self.at, self.kn = qT, kT, bT, qm, km, at, kn
                self.v, self.st, self.tails = v, st, tails
                self.items = [(None, t) for t in range(TT)] + [(m, t) for m in LEVELS for t in range(TT)]
                self.n = H * 128
                self.nb = self.n // 512

            def s(self, name):
                return S(f"decay_{name}")

            def wait(self, eng, name, count):
                eng.wait_ge(S(f"decay_{name}"), count + (0 if self.first else self.TOTAL[name]))

            TOTAL = dict(scores=14, keys=13, selected=14, decays=14, exponents=13, tail_keys=1, keys_back=1, keys_rows=1,
                         updates=1, states=1, outputs=1)

            def banks(self, it):
                b = 2 * (it % 4)
                return PS[:, b:b + self.nb, :].rearrange("p b n -> p (b n)")

            def halves(self, x, t, m):
                v = x[:, t, :].rearrange("p (g w m) -> p g w m", w=2, m=m)
                return v[:, :, 0, :], v[:, :, 1, :]

            def pe(self, pe):
                H, dk, dv = self.H, self.dk, self.dv
                self.wait(pe, "keys", 1)
                for it, (m, t) in enumerate(self.items):
                    if m:
                        self.wait(pe, "keys", it)
                    if it >= 4:
                        self.wait(pe, "selected", it - 3)
                    q, k = (self.qm, self.km) if m else (self.qT, self.kT)
                    o = self.banks(it)
                    for h in range(H):
                        hs = slice(128 * h, 128 * h + 128)
                        mm = nc.tensor.matmul(o[:, hs], k[:, t, hs], q[:, t, hs], start=True, stop=True)
                    mm.then_inc(self.s("scores"), 1)
                self.wait(pe, "tail_keys", 1)
                for t in range(TT):
                    for h in range(H):
                        e = t * H + h
                        tr = nc.tensor.transpose(PS[:, e // 4, (e % 4) * dk:(e % 4) * dk + dk],
                                                 self.km[:, t, 128 * h:128 * h + 128], CF[0:dk, 0, 0:dk])
                tr.then_inc(self.s("keys_back"), 1)
                self.wait(pe, "keys_rows", 1)
                per = 512 // dv
                for c in range(3):
                    t, r = divmod(c, 2)
                    rs = slice(64 * r, 64 * r + 64)
                    for h in range(H):
                        e = c * H + h
                        mm = nc.tensor.matmul(PS[0:dk, e // per, (e % per) * dv:(e % per) * dv + dv],
                                              self.kn[rs, t, dk * h:dk * h + dk], self.v(t, h)[rs, :], start=True, stop=True)
                mm.then_inc(self.s("updates"), 1)
                self.wait(pe, "states", 1)
                for t in range(TT):
                    for h in range(H):
                        e = t * H + h
                        o = PS[:, e // per, (e % per) * dv:(e % per) * dv + dv]
                        for r in range(2):
                            c, rs = 2 * t + r, slice(64 * r, 64 * r + 64)
                            cs = slice(128 * h + 64 * r, 128 * h + 64 * r + 64)
                            mm = nc.tensor.matmul(o[rs, :], self.at[:, t, cs], self.v(t, h), start=True, stop=(c == 0))
                            if c:
                                mm = nc.tensor.matmul(o[rs, :], self.qm[:, t, cs], self.st[c - 1][:, dv * h:dv * h + dv],
                                                      start=False, stop=True)
                mm.then_inc(self.s("outputs"), 1)

            def act(self, act):
                for it, (m, t) in enumerate(self.items):
                    if m:
                        self.wait(act, "exponents", it - 1)
                        q, k = self.halves(self.qm, t, m)[1], self.halves(self.km, t, m)[0]
                        act.activation(q, q, ACT.Exp)
                        act.activation(k, k, ACT.Exp).then_inc(self.s("decays"), 1)
                n = len(self.items)
                self.wait(act, "exponents", n - 1)
                for t in range(TT):
                    act.activation(self.qm[:, t, :], self.bT[:, t, :], ACT.Exp)
                    act.activation(self.km[:, t, :], self.km[:, t, :], ACT.Exp)
                    act.activation(self.tails[:, t, :],
                                   self.bT[:, t, :].rearrange("p (g n) -> p g n", n=CH)[:, :, CH - 1], ACT.Exp).then_inc(
                                       self.s("decays"), 1)

            def dve(self, dve, meanwhile=lambda n: None):
                n, H, dk, dv = len(self.items), self.H, self.dk, self.dv
                link = Chain(dve)

                def diff(it):
                    m, t = self.items[it]
                    if it >= 4:
                        self.wait(dve, "scores", it - 1)
                    (ql, qr), (kl, kr) = self.halves(self.qm, t, m), self.halves(self.km, t, m)
                    bl, br = self.halves(self.bT, t, m)
                    ref = bl[:, :, m - 1:m].to_broadcast(list(bl.shape))
                    dve.tensor_tensor(qr, br, ref, ALU.subtract)
                    dve.tensor_tensor(kl, ref, bl, ALU.subtract).then_inc(self.s("exponents"), 1)

                def mul(it):
                    m, t = self.items[it]
                    self.wait(dve, "decays", it - 1)
                    q, k = self.halves(self.qm, t, m)[1], self.halves(self.km, t, m)[0]
                    dve.tensor_tensor(q, q, self.halves(self.qT, t, m)[1], ALU.mult)
                    dve.tensor_tensor(k, k, self.halves(self.kT, t, m)[0], ALU.mult).then_inc(self.s("keys"), 1)

                def select(it):
                    m, t = self.items[it]
                    mask = CM[:, 0 if m is None else 1 + LEVELS.index(m), :].unsqueeze(1).to_broadcast([128, H, 128])
                    self.wait(dve, "scores", it + 1)
                    if it >= 2:
                        self.wait(dve, "selected", it - 1)
                    dve.copy_predicated(self.at[:, t, :].rearrange("p (h n) -> p h n", h=H), mask,
                                        self.banks(it).rearrange("p (h n) -> p h n", h=H)).then_inc(self.s("selected"), 1)

                dve.memset(self.at, 0.0).then_inc(self.s("keys"), 1)
                self.wait(dve, "keys", 1)
                diff(2)
                select(0)
                for it in range(2, n):
                    mul(it)
                    if it + 1 < n:
                        diff(it + 1)
                    select(it - 1)
                select(n - 1)
                for t in range(TT):
                    b = self.bT[:, t, :].rearrange("p (g n) -> p g n", n=CH)
                    last = dve.tensor_tensor(self.km[:, t, :].rearrange("p (g n) -> p g n", n=CH),
                                             b[:, :, CH - 1:CH].to_broadcast(list(b.shape)), b, ALU.subtract)
                last.then_inc(self.s("exponents"), 1)
                self.wait(dve, "decays", n)
                for t in range(TT):
                    dve.tensor_tensor(self.km[:, t, :], self.km[:, t, :], self.kT[:, t, :], ALU.mult)
                    last = dve.tensor_tensor(self.qm[:, t, :], self.qm[:, t, :], self.qT[:, t, :], ALU.mult)
                last.then_inc(self.s("tail_keys"), 1)
                meanwhile(0)
                self.wait(dve, "keys_back", 1)
                for t in range(TT):
                    for b0 in range(0, H, 4):
                        last = dve.tensor_copy(self.kn[:, t, dk * b0:dk * b0 + 4 * dk], PS[:, (t * H + b0) // 4, 0:4 * dk])
                last.then_inc(self.s("keys_rows"), 1)
                meanwhile(1)
                self.wait(dve, "updates", 1)
                per = 512 // dv
                for c in range(3):
                    for h in range(H):
                        e = c * H + h
                        new = PS[0:dk, e // per, (e % per) * dv:(e % per) * dv + dv]
                        dst = self.st[c][:, dv * h:dv * h + dv]
                        if c == 0:
                            last = dve.tensor_copy(dst, new)
                        else:
                            t, r = divmod(c, 2)
                            last = dve.scalar_tensor_tensor(
                                out=dst, in0=self.st[c - 1][:, dv * h:dv * h + dv],
                                scalar=self.tails[:, t, 2 * h + r:2 * h + r + 1], in1=new, op0=ALU.mult, op1=ALU.add)
                    if c < 2:
                        link(last)
                last.then_inc(self.s("states"), 1)

        def dve_heads(dve, link, name, o, sq, e, w, H, dv, stat):
            for t in range(TT):
                last = dve.tensor_tensor(sq[t], o[t], o[t], ALU.mult)
            link(last)
            for t in range(TT):
                last = dve.tensor_reduce(stat[:, H * t:H * t + H], sq[t], AX, ALU.add)
            link(last)
            dve_rstd(dve, name, stat=stat, n=dv)
            for t in range(TT):
                dve.tensor_tensor(e[t], e[t], w.unsqueeze(1).to_broadcast([128, H, dv]), ALU.mult)
                last = dve.tensor_tensor(o[t], o[t], stat[:, H * t:H * t + H].unsqueeze(2).to_broadcast([128, H, dv]),
                                         ALU.mult)
            link(last)
            for t in range(TT):
                last = dve.tensor_tensor(o[t], o[t], e[t], ALU.mult)
            return last

        def cols(x, c0, n=GRP):
            return x[:, :, c0:c0 + n]

        Lb = [LB[:, j, :].rearrange("p (t n) -> p t n", t=TT) for j in range(4)]
        Lh = [LB[:, j, :].rearrange("p (h n) -> p h n", h=H1) for j in range(4)]
        PQ, PA, PV1, PG1 = (cols(P, GRP * j) for j in range(4))
        G0, G1, G2, PG2 = (cols(P, GRP * (4 + j)) for j in range(4))
        F1, F2, F3 = PA, PV1, PG1
        TAILS = SM[:, 32:64].rearrange("p (t g) -> p t g", t=TT)
        TAILS2 = SM[:, 64:96].rearrange("p (t h r) -> p t h r", t=TT, h=H1)
        STAT = SM[:, 96:112]
        HG = Decay(True, H1, DH, DH, Lb[0], Lb[1], Lb[2], PQ, Lb[3], PA, Lb[1],
                   lambda t, h: P[:, t, 2 * GRP + DH * h:2 * GRP + DH * h + DH],
                   [LB[:, 0, 0:GRP], LB[:, 0, GRP:2 * GRP], LB[:, 2, 0:GRP]], TAILS)

        def bank_cols(b0, nb):
            return PS[:, b0:b0 + nb, :].rearrange("p b n -> p (b n)")

        def entry(b0, e):
            return PS[:, b0 + e // 4, 128 * (e % 4):128 * (e % 4) + 128]

        def heads3(x, t, H=H1):
            return x[:, t, :].rearrange("p (h n) -> p h n", h=H)

        CONV_UNIT = (1, 4, 7, 10)

        def conv_fns(n):
            r0, c0 = round_of["conv"] + 4 * n, (4 + n) * GRP

            def pe_x(x):
                return lambda pe: pe_round(pe, r0 + x, P, 2 * x, 2, f0=c0)

            def dve_x(x):
                def f(dve):
                    link = Chain(dve)
                    dve.wait_ge(S("round_ready"), r0 + x + 1)
                    for tap in (3, 2, 1, 0):
                        for j in range(2):
                            sh, blk = 3 - tap, 8 * n + 2 * x + j
                            w = COLS[:, 24 * tap + blk:24 * tap + blk + 1]
                            src = PS[:, 4 + (r0 + x) % 4, 256 * j:256 * j + T - sh]
                            dst = P[:, j, c0 + 256 * x + sh:c0 + 256 * x + T]
                            if sh == 0:
                                last = dve.tensor_scalar(dst, src, w, None, ALU.mult)
                            else:
                                last = dve.scalar_tensor_tensor(out=dst, in0=src, scalar=w, in1=dst, op0=ALU.mult,
                                                                op1=ALU.add)
                        if tap:
                            link(last)
                        else:
                            last.then_inc(S("round_free"), 1)
                return f

            def spread(make):
                return [make(CONV_UNIT.index(k)) if k in CONV_UNIT else None for k in range(CONV_UNIT[-1] + 1)]
            return dict(pe=spread(pe_x), dve=spread(dve_x))

        def pe_mix1(pe):
            for b in range(4):
                pe.wait_ge(S(f"bank_free{b}"), MIX1.at["done"][b])
            pe.wait_ge(S("ada_used"), ADA_IN)
            for b in range(8):
                mm = nc.tensor.matmul(PS[:, b % 8, :], ONES, MOD[:, b // 4, 512 * (b % 4):512 * (b % 4) + 512],
                                      start=True, stop=True)
                if b % 4 == 3:
                    mm.then_inc(S("mod_summed"), 1)
            pe.wait_ge(S("mod_copied"), 2)
            for src, b0 in ((PA, 0), (PQ, 4)):
                for t in range(TT):
                    for h in range(H1):
                        tr = nc.tensor.transpose(entry(b0, t * H1 + h), src[:, t, 128 * h:128 * h + 128], IDENT)
                tr.then_inc(S("hg_turned"), 1)
            HG.pe(pe)
            pe.wait_ge(S("hg_out"), 1)
            for n in range(2):
                pe.wait_ge(S("qk_squared"), n + 1)
                for b in range(4):
                    mm = nc.tensor.matmul(PS[:, 4 * n + b, :], ONES, LB[:, 3, 512 * b:512 * b + 512], start=True, stop=True)
                mm.then_inc(S("qk_summed"), 1)
            pe.wait_ge(S("qk_normed"), 2)
            pe.wait_ge(S("conv_silu"), 3)
            for n, src in enumerate((Lh[1], Lh[2])):
                for t in range(TT):
                    for h in range(H1):
                        tr = nc.tensor.transpose(entry(4 * n, t * H1 + h), src[:, h, 128 * t:128 * t + 128], IDENT)
                tr.then_inc(S("kv_rows"), 1)
            pe.wait_ge(S("gates_ready"), 1)
            pe.wait_ge(S("kv_copied"), 2)
            nc.tensor.matmul(PS[:, 0, 0:16], UPPER, GATES[:, 0, :], start=True, stop=True)
            nc.tensor.matmul(PS[:, 0, 16:32], AFTER, GATES[:, 0, :], start=True, stop=True).then_inc(S("sums_ready"), 1)
            for e in range(16):
                mm = nc.tensor.matmul(entry(4, e), GATES[:, 0, e:e + 1].to_broadcast([128, 128]), UPPER,
                                      start=True, stop=True)
            mm.then_inc(S("sums_ready"), 1)
            pe.wait_ge(S("sums_copied"), 1)
            for e in range(16):
                t, h = divmod(e, H1)
                k = Lh[1][:, h, 128 * t:128 * t + 128]
                mm = nc.tensor.matmul(entry(0, e), k, k, start=True, stop=True)
            mm.then_inc(S("kk_ready"), 1)
            pe.wait_ge(S("rows_exped"), 1)
            pe.wait_ge(S("gamma_made"), 1)
            for e in range(16):
                t, h = divmod(e, H1)
                tk = slice(128 * t, 128 * t + 128)
                mm = nc.tensor.matmul(entry(4, e), Lh[1][:, h, tk], Lh[0][:, h, tk], start=True, stop=True)
            mm.then_inc(S("kk_ready"), 1)
            pe.wait_ge(S("m_made"), 1)
            for e in range(16):
                t, h = divmod(e, H1)
                mm = nc.tensor.transpose(entry(0, e), F2[:, t, 128 * h:128 * h + 128], IDENT)
            mm.then_inc(S("m_turned"), 1)
            for it in range(2 * (len(LEVELS) - 1)):
                t = it % 2
                pe.wait_ge(S("c_masked"), it + 1)
                for h in range(H1):
                    hs = slice(128 * h, 128 * h + 128)
                    mm = nc.tensor.matmul(entry(2 * t, h), G0[:, t, hs], Lb[2][:, t, hs], start=True, stop=True)
                mm.then_inc(S("cx_ready"), 1)
                pe.wait_ge(S("cx_copied"), it + 1)
                for h in range(H1):
                    hs = slice(128 * h, 128 * h + 128)
                    mm = nc.tensor.matmul(entry(4 + 2 * t, h), Lb[3][:, t, hs], F2[:, t, hs], start=True, stop=True)
                mm.then_inc(S("xcx_ready"), 1)
                for h in range(H1):
                    hs = slice(128 * h, 128 * h + 128)
                    mm = nc.tensor.matmul(entry(2 * t, h), F2[:, t, hs], Lb[3][:, t, hs], start=True, stop=True)
                mm.then_inc(S("xcx_ready"), 1)
            pe.wait_ge(S("rhs_ready"), 1)
            for e in range(16):
                t, h = divmod(e, H1)
                hs = slice(128 * h, 128 * h + 128)
                nc.tensor.matmul(entry(0, e), Lb[3][:, t, hs], G2[:, t, hs], start=True, stop=True)
                mm = nc.tensor.matmul(entry(4, e), F2[:, t, hs], Lb[3][:, t, hs], start=True, stop=True)
            mm.then_inc(S("uw_ready"), 1)
            for c in range(4):
                t, r = divmod(c, 2)
                rs = slice(64 * r, 64 * r + 64)
                if c:
                    pe.wait_ge(S("state_made"), c)
                    for h in range(H1):
                        mm = nc.tensor.matmul(PS[rs, h // 4, 128 * (h % 4):128 * (h % 4) + 128],
                                              Lb[1][:, t, 128 * h + 64 * r:128 * h + 64 * r + 64],
                                              G0[:, 0, 128 * h:128 * h + 128], start=True, stop=True)
                    mm.then_inc(S("ws_ready"), 1)
                pe.wait_ge(S("v_new"), c + 1)
                for h in range(H1):
                    hs = slice(128 * h, 128 * h + 128)
                    cs = slice(128 * h + 64 * r, 128 * h + 64 * r + 64)
                    o = entry(4, t * H1 + h)[rs, :]
                    if c:
                        nc.tensor.matmul(o, Lh[0][:, h, 128 * t + 64 * r:128 * t + 64 * r + 64], G0[:, 0, hs],
                                         start=True, stop=False)
                    mm = nc.tensor.matmul(o, F3[rs, t, cs], Lb[2][rs, t, hs], start=(c == 0), stop=True)
                if c == 3:
                    mm.then_inc(S("gdn_out"), 1)
                    break
                for h in range(H1):
                    hs = slice(128 * h, 128 * h + 128)
                    mm = nc.tensor.matmul(entry(2, h), G1[rs, t, hs], Lb[2][rs, t, hs], start=True, stop=True)
                mm.then_inc(S("gdn_update"), 1)
            pe_split(pe, "mix1", P, ready=(S("mix1_ready"), 1))

        def act_mix1(act):
            for comp in range(2):
                act.wait_ge(S("mod_summed"), comp + 1)
                act.activation(MOD[:, comp, :], bank_cols(4 * comp, 4), ACT.Copy).then_inc(S("mod_copied"), 1)
            act.wait_ge(S("hg_turned"), 1)
            act.activation(LB[:, 1, :], bank_cols(0, 4), ACT.Sigmoid).then_inc(S("hg_pre"), 1)
            act.wait_ge(S("hg_turned"), 2)
            act.activation(LB[:, 0, :], bank_cols(4, 4), ACT.Copy).then_inc(S("hg_pre"), 1)
            act.wait_ge(S("hg_f"), 1)
            act.activation(LB[:, 3, :], LB[:, 2, :], ACT.Ln).then_inc(S("hg_pre"), 1)
            HG.act(act)
            act.wait_ge(S("decay_states"), 1)
            for t in range(TT):
                act.activation(Lb[3][:, t, :], PG1[:, t, :], ACT.Silu).then_inc(S("hg_gate"), 1)
            act.wait_ge(S("decay_outputs"), 1)
            for n in (0, 2, 1):
                if n == 1:
                    act.wait_ge(S("hg_out"), 2)
                for j in range(2):
                    c0 = (4 + n) * GRP
                    last = act.activation(Lh[n].rearrange("p (x j) t -> p x j t", j=2)[:, :, j, :],
                                          P[:, j, c0:c0 + GRP].rearrange("p (x t) -> p x t", t=T), ACT.Silu)
                last.then_inc(S("conv_silu"), 1)
            for n in range(2):
                act.wait_ge(S("qk_summed"), n + 1)
                act.activation(LB[:, 3, :], bank_cols(4 * n, 4), ACT.Ln, bias=EPS_COL).then_inc(S("qk_ln"), 1)
                act.wait_ge(S("qk_ln"), n + 1)
                act.activation(LB[:, 3, :], LB[:, 3, :], ACT.Exp, scale=-0.5).then_inc(S("qk_rstd"), 1)
            act.wait_ge(S("gate_args"), 1)
            act.activation(GATES[:, 1, :], GATES[:, 1, :], ACT.Exp, scale=-1.0)
            act.activation(GATES[:, 2, :], GATES[:, 2, :], ACT.Exp, scale=-1.0)
            act.activation(ROWS[:, 280:288], ROWS[:, 256:264], ACT.Exp).then_inc(S("gate_exps"), 1)
            act.wait_ge(S("gate_exps"), 1)
            act.activation(GATES[:, 1, :], GATES[:, 1, :], ACT.Ln, bias=ONE_COL).then_inc(S("gate_exps"), 1)
            for n, dst in enumerate((G1, G2)):
                act.wait_ge(S("kv_rows"), n + 1)
                for t in range(TT):
                    last = act.activation(dst[:, t, :], bank_cols(4 * n + 2 * t, 2), ACT.Copy)
                last.then_inc(S("kv_copied"), 1)
            act.wait_ge(S("sums_copied"), 1)
            act.activation(GATES[:, 5:7, :], GATES[:, 3:5, :], ACT.Exp).then_inc(S("sum_exps"), 1)
            act.wait_ge(S("sums_ready"), 2)
            act.wait_ge(S("qk_normed"), 2)
            for t in range(TT):
                last = act.activation(G0[:, t, :], bank_cols(4 + 2 * t, 2), ACT.Exp)
            last.then_inc(S("rows_exped"), 1)
            act.wait_ge(S("gamma_made"), 1)
            for t in range(TT):
                act.activation(F3[:, t, :], F3[:, t, :], ACT.Exp)
                last = act.activation(F2[:, t, :], F2[:, t, :], ACT.Exp, scale=-1.0)
            last.then_inc(S("gamma_exped"), 1)
            act.wait_ge(S("m_turned"), 1)
            act.activation(LB[:, 1, :], bank_cols(0, 4), ACT.Copy).then_inc(S("mt_copied"), 1)
            for it in range(2 * (len(LEVELS) - 1)):
                t = it % 2
                act.wait_ge(S("cx_ready"), it + 1)
                act.activation(F2[:, t, :], bank_cols(2 * t, 2), ACT.Copy).then_inc(S("cx_copied"), 1)
            act.wait_ge(S("uw_ready"), 1)
            act.activation(LB[:, 2, :], bank_cols(0, 4), ACT.Copy).then_inc(S("u_copied"), 1)
            act.activation(LB[:, 1, :], bank_cols(4, 4), ACT.Copy).then_inc(S("w_copied"), 1)
            for t in range(TT):
                act.activation(Lb[3][:, t, :], PG2[:, t, :], ACT.Silu).then_inc(S("gdn_gate"), 1)
            act_split(act, "mix1", LH2)

        EPS_COL, ONE_COL = SM[:, 236:237], SM[:, 237:238]

        MIX1 = next(c for _, cs in segs for c in cs if c.phase == "mix1")
        ADA_IN = 2 * KT + 4 * KT
        MIX_LOAD = MIX1.load_of(1) + 1

        def ada_mix(dve, first, count):
            for kt in range(first, first + count):
                m = MIX_LOAD + kt
                dve.wait_ge(S(f"weights_in{m % RAWN}"), 16 * (m // RAWN + 1))
                ada_step(dve, MOD[:, 2, :], RAW[:, m % RAWN, :, :].rearrange("p j n -> p (j n)"), kt, ADA_IN + kt)

        def dve_mix1(dve):
            link = Chain(dve)
            dve.memset(EPS_COL, EPS)
            link(dve.memset(ONE_COL, 1.0))
            dve.wait_ge(S("hg_pre"), 1)
            for h in range(H1):
                hs = slice(128 * h, 128 * h + 128)
                last = dve.tensor_scalar(Lb[2][:, :, hs], Lb[1][:, :, hs], COLS[:, 104 + h:105 + h], COLS[:, 96 + h:97 + h],
                                         ALU.mult, ALU.add)
            last.then_inc(S("hg_f"), 1)
            dve.wait_ge(S("hg_f"), 1)
            link(dve.tensor_scalar(LB[:, 1, :], LB[:, 2, :], -1.0, 1.0, ALU.mult, ALU.add))
            dve.wait_ge(S("hg_pre"), 3)
            for g in range(TT * GRP // CH):
                gs = slice(CH * g, CH * g + CH)
                last = dve.tensor_tensor_scan(out=LB[:, 2, gs], data0=ONES[:, 0:CH], data1=LB[:, 3, gs], initial=0.0,
                                              op0=ALU.mult, op1=ALU.add)
            link(last)
            HG.dve(dve, lambda n: ada_mix(dve, n, 1))
            ada_mix(dve, 2, 1)
            dve.wait_ge(S("decay_outputs"), 1)
            for t in range(TT):
                last = dve.tensor_copy(PQ[:, t, :], bank_cols(2 * t, 2))
            last.then_inc(S("hg_out"), 1)
            dve.wait_ge(S("hg_out"), 1)
            dve.wait_ge(S("hg_gate"), 2)
            dve.wait_ge(S("rows_in"), 16 * len(ROW_VECTORS))
            dve_heads(dve, link, "hg_heads", *([heads3(x, t) for t in range(TT)] for x in (PQ, Lb[1], Lb[3])),
                      ROWS[:, 0:128], H1, DH, STAT).then_inc(S("hg_out"), 1)
            dve.wait_ge(S("hg_out"), 2)
            for n in range(2):
                dve.wait_ge(S("conv_silu"), 1 + 2 * n)
                dve.tensor_tensor(LB[:, 3, :], LB[:, n, :], LB[:, n, :], ALU.mult).then_inc(S("qk_squared"), 1)
                ada_mix(dve, 3 + 2 * n, 2 - n)
                dve.wait_ge(S("qk_rstd"), n + 1)
                dve.scalar_tensor_tensor(out=LB[:, n, :], in0=LB[:, n, :], scalar=DH ** -0.5 if n == 0 else 1.0,
                                         in1=LB[:, 3, :], op0=ALU.mult, op1=ALU.mult).then_inc(S("qk_normed"), 1)
                dve.wait_ge(S("qk_normed"), n + 1)
            g = [GATES[:, j, :] for j in range(10)]
            g3 = [GATES[:, j, :].rearrange("p (t h) -> p t h", t=TT) for j in range(10)]

            def on_heads(c0):
                return ROWS[:, c0:c0 + H1].unsqueeze(1).to_broadcast([128, TT, H1])
            link(dve.tensor_tensor(g3[0], P[:, :, 8 * GRP:8 * GRP + H1], on_heads(264), ALU.add))
            link(dve.tensor_scalar(g[8], g[0], -1.0, None, ALU.mult))
            link(dve.tensor_tensor(g[1], g[0], g[8], ALU.max))
            dve.tensor_copy(g3[2], P[:, :, 8 * GRP + H1:8 * GRP + 2 * H1]).then_inc(S("gate_args"), 1)
            link(dve.tensor_scalar(g[0], g[0], 0.0, None, ALU.max))
            dve.wait_ge(S("gate_exps"), 2)
            link(dve.tensor_tensor(g[0], g[0], g[1], ALU.add))
            link(dve.tensor_tensor(g3[0], g3[0], on_heads(280), ALU.mult))
            dve.tensor_scalar(g[0], g[0], -1.0, None, ALU.mult).then_inc(S("gates_ready"), 1)
            link(dve.tensor_scalar(g[2], g[2], 1.0, None, ALU.add))
            link(dve.reciprocal(g[7], g[2]))
            ada_mix(dve, 6, 4)
            dve.wait_ge(S("sums_ready"), 1)
            dve.tensor_copy(GATES[:, 3:5, :], PS[:, 0, 0:32].rearrange("p (a b) -> p a b", a=2)).then_inc(S("sums_copied"), 1)
            dve.wait_ge(S("sums_copied"), 1)
            dve.wait_ge(S("sums_ready"), 2)
            dve.wait_ge(S("rows_exped"), 1)
            for e in range(16):
                t, h = divmod(e, H1)
                hs = slice(128 * h, 128 * h + 128)
                dve.tensor_scalar(F3[:, t, hs], entry(4, e), g[3][:, e:e + 1], 0.0, ALU.subtract, ALU.min)
                last = dve.tensor_scalar(F2[:, t, hs], entry(4, e), g[3][:, e:e + 1], 0.0, ALU.subtract, ALU.max)
            last.then_inc(S("gamma_made"), 1)
            dve.wait_ge(S("sum_exps"), 1)
            link(dve.tensor_tensor(g[8], g[7], g[5], ALU.mult))
            link(dve.tensor_copy(TAILS2, G0.rearrange("p t (h r n) -> p t h r n", h=H1, r=2)[:, :, :, :, CH - 1]))
            dve.wait_ge(S("gamma_exped"), 1)
            for t in range(TT):
                dve.tensor_tensor(heads3(F3, t), heads3(F3, t), UPPER.unsqueeze(1).to_broadcast([128, H1, 128]), ALU.mult)
                last = dve.tensor_tensor(heads3(F2, t), heads3(F2, t), AFTER.unsqueeze(1).to_broadcast([128, H1, 128]),
                                         ALU.mult)
            link(last)
            dve.wait_ge(S("kk_ready"), 1)
            for e in range(16):
                t, h = divmod(e, H1)
                hs = slice(128 * h, 128 * h + 128)
                last = dve.scalar_tensor_tensor(out=F2[:, t, hs], in0=entry(0, e), scalar=g[7][:, e:e + 1],
                                                in1=F2[:, t, hs], op0=ALU.mult, op1=ALU.mult)
            last.then_inc(S("m_made"), 1)
            dve.wait_ge(S("m_made"), 1)
            dve.wait_ge(S("kk_ready"), 2)
            for t in range(TT):
                dve.tensor_tensor(F3[:, t, :], F3[:, t, :], bank_cols(4 + 2 * t, 2), ALU.mult)
                q = Lh[0][:, :, 128 * t:128 * t + 128]
                last = dve.tensor_tensor(q, q, heads3(G0, t), ALU.mult)
            link(last)

            def bc(mat):
                return mat.unsqueeze(1).to_broadcast([128, H1, 128])
            dve.wait_ge(S("mt_copied"), 1)
            for t in range(TT):
                dve.tensor_tensor(heads3(Lb[2], t), heads3(F2, t), bc(CM[:, 7, :]), ALU.mult)
                last = dve.tensor_tensor(heads3(Lb[3], t), heads3(Lb[1], t), bc(CM[:, 1, :]), ALU.mult)
            link(last)
            for t in range(TT):
                dve.scalar_tensor_tensor(out=heads3(Lb[2], t), in0=heads3(Lb[2], t), scalar=-1.0, in1=bc(IDENT),
                                         op0=ALU.mult, op1=ALU.add)
                last = dve.scalar_tensor_tensor(out=heads3(Lb[3], t), in0=heads3(Lb[3], t), scalar=-1.0, in1=bc(IDENT),
                                                op0=ALU.mult, op1=ALU.add)
            link(last)

            def mask_c(it):
                lv, t = divmod(it, 2)
                dve.tensor_tensor(heads3(G0, t), heads3(Lb[1], t), bc(CM[:, 2 + lv, :]), ALU.mult).then_inc(S("c_masked"), 1)
            mask_c(0)
            mask_c(1)
            n_it = 2 * (len(LEVELS) - 1)
            for it in range(n_it):
                t = it % 2
                dve.wait_ge(S("xcx_ready"), 2 * it + 1)
                dve.tensor_tensor(Lb[2][:, t, :], Lb[2][:, t, :], bank_cols(4 + 2 * t, 2), ALU.subtract)
                dve.wait_ge(S("xcx_ready"), 2 * it + 2)
                last = dve.tensor_tensor(Lb[3][:, t, :], Lb[3][:, t, :], bank_cols(2 * t, 2), ALU.subtract)
                link(last)
                if it + 2 < n_it:
                    mask_c(it + 2)

            def scaled(dst, src, col, t):
                return dve.tensor_tensor(heads3(dst, t), heads3(src, t),
                                         g[col][:, H1 * t:H1 * t + H1].unsqueeze(2).to_broadcast([128, H1, 128]), ALU.mult)
            for t in range(TT):
                scaled(G2, G2, 7, t)
                last = scaled(F2, G1, 8, t)
            last.then_inc(S("rhs_ready"), 1)
            dve.wait_ge(S("rhs_ready"), 1)
            for t in range(TT):
                last = scaled(G1, G1, 6, t)
            link(last)
            ada_mix(dve, 10, 3)
            dve.wait_ge(S("u_copied"), 1)
            dve.wait_ge(S("w_copied"), 1)
            for c in range(4):
                t, r = divmod(c, 2)
                rs = slice(64 * r, 64 * r + 64)
                if c == 0:
                    dve.memset(SM[:, 238:239], 0.0).then_inc(S("v_new"), 1)
                else:
                    ada_mix(dve, 12 + c, 1)
                    dve.wait_ge(S("ws_ready"), c)
                    dve.tensor_tensor(Lb[2][rs, t, :], Lb[2][rs, t, :], PS[rs, 0:2, :].rearrange("p b n -> p (b n)"),
                                      ALU.subtract).then_inc(S("v_new"), 1)
                if c == 3:
                    break
                dve.wait_ge(S("gdn_update"), c + 1)
                for h in range(H1):
                    hs = slice(128 * h, 128 * h + 128)
                    if c == 0:
                        last = dve.tensor_copy(G0[:, 0, hs], entry(2, h))
                    else:
                        last = dve.scalar_tensor_tensor(out=G0[:, 0, hs], in0=G0[:, 0, hs], scalar=TAILS2[:, t, h, r:r + 1],
                                                        in1=entry(2, h), op0=ALU.mult, op1=ALU.add)
                last.then_inc(S("state_made"), 1)
                dve.wait_ge(S("state_made"), c + 1)
            dve.wait_ge(S("gdn_out"), 1)
            for t in range(TT):
                last = dve.tensor_copy(F1[:, t, :], bank_cols(4 + 2 * t, 2))
            link(last)
            dve.wait_ge(S("gdn_gate"), 2)
            dve_heads(dve, link, "gdn_heads", *([heads3(x, t) for t in range(TT)] for x in (F1, F2, Lb[3])),
                      ROWS[:, 128:256], H1, DH, STAT).then_inc(S("mix1_ready"), 1)
            dve_split(dve, "mix1", LH2, LL2)

        def pool_mix1(pool):
            pool_rstd(pool, "hg_heads", STAT)
            pool_rstd(pool, "gdn_heads", STAT)

        VEC2 = NAT[:, :, :].rearrange("p t n -> p (t n)")
        TURNED = ("hid1", "hid2")

        def dve_residual(dve, link, name, coef):
            for t in range(TT):
                dve_rstd(dve, name, t)
                link(dve.scalar_tensor_tensor(out=Y[:, t, :], in0=Y[:, t, :], scalar=rstd(name, t), in1=coef,
                                              op0=ALU.mult, op1=ALU.mult))
                dve.tensor_tensor(X[:, t, :], X[:, t, :], Y[:, t, :], ALU.add).then_inc(S("rows_ready"), 1)

        def dve_rows_ready(dve):
            for t in range(TT):
                dve.memset(SM[:, 232 + t:233 + t], 0.0).then_inc(S("rows_ready"), 1)

        def dve_norm_rows(dve, link, name, dst, src, w, shift=None):
            for t in range(TT):
                dve_rstd(dve, name, t)
                for c0, c1 in ((0, D),) if t < TT - 1 else ((0, D // 2), (D // 2, D)):
                    last = dve.scalar_tensor_tensor(out=dst[:, t, c0:c1], in0=src[:, t, c0:c1], scalar=rstd(name, t),
                                                    in1=w[:, c0:c1], op0=ALU.mult, op1=ALU.mult)
                    if shift is not None:
                        link(last)
                        last = dve.tensor_tensor(dst[:, t, c0:c1], dst[:, t, c0:c1], shift[:, c0:c1], ALU.add)
                    if t == TT - 1:
                        last.then_inc(S("h_ready"), 1)

        def pool_norm_ffn1(pool):
            pool.wait_ge(S("round_ready"), round_of["mix1"] + 8)
            pool.dma_start(X[:, :, :], a["x"].rearrange("(t p) d -> p t d", p=128)).then_inc(S("x2_in"), 16)
            pool.dma_start(VEC[:, :], row_vector("post_mix_norm")).then_inc(S("vecs_in"), 16)
            pool.dma_start(VEC2, row_vector("pre_ffn_norm")).then_inc(S("vecs_in"), 16)
            pool_rstd(pool, "post_mix")
            pool_rstd(pool, "pre_ffn")

        def act_norm_ffn1(act):
            act_squares(act, "post_mix", Y)
            act_squares(act, "pre_ffn", X)
            act_split(act, "norm_ffn1", LH2)

        def pe_mod_sum(pe, name, row, steps):
            pe.wait_ge(S("ada_used"), steps)
            for b in range(4):
                pe.wait_ge(S(f"bank_free{b}"), AT[name]["done"][b])
                mm = nc.tensor.matmul(PS[:, b, :], ONES, MOD[:, row, 512 * b:512 * b + 512], start=True, stop=True)
            mm.then_inc(S("mod_summed"), 1)

        def pe_norm_ffn1(pe):
            pe_mod_sum(pe, "norm_ffn1", 2, ADA_IN + KT)
            pe_split(pe, "norm_ffn1", Y, ready=(S("h_ready"), 3))

        def dve_norm_ffn1(dve):
            link = Chain(dve)
            for b in range(4):
                dve.wait_ge(S(f"bank_free{b}"), AT["norm_ffn1"]["done"][b])
            dve_rows_ready(dve)
            dve.wait_ge(S("vecs_in"), 32)
            dve.wait_ge(S("x2_in"), 16)
            dve.tensor_tensor(MOD[:, 0, :], MOD[:, 0, :], VEC[:, :], ALU.mult)
            dve.wait_ge(S("mod_summed"), 3)
            link(dve.scalar_tensor_tensor(out=MOD[:, 2, :], in0=bank_cols(0, 4), scalar=1.0, in1=VEC2, op0=ALU.add,
                                          op1=ALU.mult))
            dve_residual(dve, link, "post_mix", MOD[:, 0, :])
            dve_norm_rows(dve, link, "pre_ffn", Y, X, MOD[:, 2, :], MOD[:, 1, :])
            dve_split(dve, "norm_ffn1", LH2, LL2)
            dve.memset(Y[:, :, :], 0.0).then_inc(S("y_cleared"), 1)
            dve.wait_ge(S("y_cleared"), 1)

        def hid1_fns(nk):
            def pe_j(j):
                def f(pe, c, i):
                    base, step = HID[id(c)], 4 if i is not None else 0
                    if j == 0:
                        pe.wait_ge(S("hid_squared"), val(4 * base + 4, 4 if i is not None else 0, i))
                    pe_round(pe, round_of["hid1"] + 4 * base + j, NAT, 2 * j, 2, i, step)
                return f

            def act_j(j):
                def f(act, c, i):
                    act_round(act, round_of["hid1"] + 4 * HID[id(c)] + j, L2H, 2 * j, 2, i, 4 if i is not None else 0)
                return f

            def dve_j(j):
                def f(dve, c, i):
                    r = 4 * HID[id(c)] + j
                    st = 4 if i is not None else 0
                    dve_round(dve, round_of["hid1"] + r, L2H, L2L, 2 * j, 2, nhigh_of["hid1"] + r + 1, i, st, st)
                return f
            return dict(pe=[pe_j(j) for j in range(4)], act=[act_j(j) for j in range(4)], dve=[dve_j(j) for j in range(4)])

        HID, AT = {}, {}
        for iters, chunks in segs:
            for c in chunks:
                if c.phase and c.phase not in ("none", "hid_wait"):
                    AT.setdefault(c.phase, c.at)
        hid1_turns = [c for _, cs in segs for c in cs if c.phase == "hid1"]
        for n, c in enumerate(hid1_turns):
            HID[id(c)] = n

        def wait_hid(pe, c, i):
            r = ROUNDS_BEFORE[id(c)]
            pe.wait_ge(S("round_free"), val(r[0], r[1] if i is not None else 0, i))

        ROUNDS_BEFORE = {}
        waits1 = [c for _, cs in segs for c in cs if c.phase == "hid_wait" and c.w is a["w_ff2"]]
        for n, c in enumerate(waits1):
            ROUNDS_BEFORE[id(c)] = (round_of["hid1"] + 4 * (1 if n == 0 else 7), 4)

        def last_hid1():
            def pe_f(pe):
                pe.wait_ge(S("hid_squared"), 32)
                for j in range(4):
                    pe_round(pe, round_of["hid1_last"] + j, NAT, 2 * j, 2)
                pe.wait_ge(S("round_free"), round_of["hid1_last"] + 4)

            def act_f(act):
                for j in range(4):
                    act_round(act, round_of["hid1_last"] + j, L2H, 2 * j, 2)

            def dve_f(dve):
                for j in range(4):
                    dve_round(dve, round_of["hid1_last"] + j, L2H, L2L, 2 * j, 2, nhigh_of["hid1_last"] + j + 1)
            return dict(pe=[pe_f], act=[act_f], dve=[dve_f])

        def dve_y_whole(dve, name):
            for b in range(4):
                dve.wait_ge(S(f"bank_free{b}"), AT[name]["done"][b])

        def pool_norm_in2(pool):
            pool.wait_ge(S("h_ready"), 3)
            pool.dma_start(VEC[:, :], row_vector("post_ffn_norm")).then_inc(S("vecs_in"), 16)
            pool.wait_ge(S("round_ready"), round_of["hid1_last"] + 4)
            pool.dma_start(VEC2, row_vector("norm_mix_2")).then_inc(S("vecs_in"), 16)
            pool_rstd(pool, "post_ffn")
            pool_rstd(pool, "mix_in")

        def act_norm_in2(act):
            act_squares(act, "post_ffn", Y)
            act_squares(act, "mix_in", X)
            act_split(act, "norm_in2", LH2)

        def pe_norm_in2(pe):
            pe_mod_sum(pe, "norm_in2", 3, ADA_IN + 3 * KT)
            pe_split(pe, "norm_in2", Y, ready=(S("h_ready"), 5))

        def dve_norm_in2(dve):
            link = Chain(dve)
            dve_y_whole(dve, "norm_in2")
            dve_rows_ready(dve)
            dve.wait_ge(S("vecs_in"), 64)
            dve.wait_ge(S("mod_summed"), 4)
            link(dve.tensor_tensor(MOD[:, 3, :], bank_cols(0, 4), VEC[:, :], ALU.mult))
            dve_residual(dve, link, "post_ffn", MOD[:, 3, :])
            dve_norm_rows(dve, link, "mix_in", Y, X, VEC2)
            dve_split(dve, "norm_in2", LH2, LL2)

        SH = AH + BH
        NA = AH * HD
        QA, KA, VA, QB, KB, VB = 0, NA, 2 * NA, 3 * NA, 3 * NA + BH * HD, 3 * NA + 2 * BH * HD
        FL = 3 * NA + 3 * BH * HD
        QC, KC = FL + BH, FL + BH + CH2 * CK
        VC = KC + CH2 * CK
        RC = VC + CH2 * CV
        GL = RC + CH2 * CV
        LBF = LB[:, :, :].rearrange("p j n -> p (j n)")
        QKT = LBF[:, 0:20 * T].rearrange("p (j t) -> p j t", t=T)
        TILES = [QA + 128 * j for j in range(6)] + [KA + 128 * j for j in range(6)] + \
                [QB + 128 * j for j in range(4)] + [KB + 128 * j for j in range(4)]
        BIASA = LBF[:, 20 * T:20 * T + AH * 256].rearrange("p (h x) -> p h x", h=AH)
        OR = MODF[:, 0:2 * D].rearrange("p (t d) -> p t d", t=TT)
        BIASB = MODF[:, 2 * D:2 * D + BH * 384].rearrange("p (h x) -> p h x", h=BH)
        W2 = MODF[0:16, 3 * D + 1024:3 * D + 1408]
        GLT = MODF[0:16, 3 * D + 1408:3 * D + 1664]
        ER = P2[:, 0, 0:1152].rearrange("p (r x) -> p r x", r=3)
        PTR = P2[:, 1, 0:1152].rearrange("p (r x) -> p r x", r=3)
        MAXES, SUMS = SM[:, 112:120], SM[:, 120:128]

        def head_tiles(h):
            if h < AH:
                return h // 2, 6 + h // 2, 64 * (h % 2), VA + HD * h
            j = h - AH
            return 12 + j // 2, 16 + j // 2, 64 * (j % 2), VB + HD * j

        CT4 = [x.rearrange("p (t n) -> p t n", t=TT) for x in
               (LBF[0:CK, 0:1024], LBF[0:CK, 1024:2048], LBF[0:CK, 2048:3072], LBF[0:CK, 3072:4096],
                LBF[0:CK, 4096:5120], LBF[0:CK, 6144:7168], LBF[0:CK, 7168:8192])]
        CQT, CKT, CBT, CKM, CQM, CX, CE = CT4
        CAT = LBF[:, 5120:6144].rearrange("p (t n) -> p t n", t=TT)
        CKN = LBF[:, 6144:6144 + TT * CH2 * CK].rearrange("p (t n) -> p t n", t=TT)
        GA = Decay(False, CH2, CK, CV, CQT, CKT, CBT, CQM, CKM, CAT, CKN,
                   lambda t, h: P2[:, t, VC + CV * h:VC + CV * h + CV],
                   [MODF[0:CK, 2 * D:2 * D + 768], MODF[0:CK, 2 * D + 768:2 * D + 1536], MODF[0:CK, 3 * D:3 * D + 768]],
                   SM[0:CK, 128:144].rearrange("p (t g) -> p t g", t=TT))
        CSTAT = SM[:, 144:152]

        def pool_mix2(pool):
            pool.wait_ge(S("round_ready"), round_of["norm_in2"] + 8)
            pool.wait_ge(S("h_ready"), 5)
            pool.dma_start(W2, a["c_gate_w2_2"]).then_inc(S("w2_in"), 16)
            pool.wait_ge(S("unit_used"), AT["mix2"]["u"])
            for j in range(4):
                pool.wait_ge(S(f"table_out{j}"), 16 * (AH // 4))
            tp = a["toeplitz"]
            for h in range(AH):
                flat = tp[h, :, :].rearrange("p x -> (p x)")
                src = flat[127:127 + 128 * 383].rearrange("(p x) -> p x", x=383)[:, 0:256]
                pool.dma_start(BIASA[:, h, :], src).then_inc(S("bias_a_in"), 16)
            pool_rstd(pool, "gla_heads", CSTAT)

        def pe_mix2(pe):
            for b in range(4):
                pe.wait_ge(S(f"bank_free{b}"), AT["mix2"]["done"][b])
            pe.wait_ge(S("f_ready"), 1)
            lf = GATES[:, 0, :]
            nc.tensor.matmul(PS[:, 0, 0:8], UPPER_ALL, lf[:, 0:8], start=True, stop=True)
            nc.tensor.matmul(PS[:, 0, 8:16], ONES, lf[:, 0:8], start=True, stop=False)
            nc.tensor.matmul(PS[:, 0, 8:16], UPPER_ALL, lf[:, 8:16], start=False, stop=True).then_inc(S("c_ready"), 1)
            for h in range(BH):
                o = PS[:, 4 + h // 2, 256 * (h % 2):256 * (h % 2) + 256]
                f0, f1 = (lf[:, 8 * t + h:8 * t + h + 1].to_broadcast([128, 128]) for t in range(TT))
                nc.tensor.matmul(o[:, 0:128], f0, UPPER_ALL, start=True, stop=True)
                nc.tensor.matmul(o[:, 128:256], f0, ONES, start=True, stop=False)
                mm = nc.tensor.matmul(o[:, 128:256], f1, UPPER_ALL, start=False, stop=True)
            mm.then_inc(S("c_ready"), 1)
            for r in range(10):
                if r >= 3:
                    pe.wait_ge(S("qk2_copied"), r - 2)
                for j in range(2):
                    for t in range(TT):
                        c0 = TILES[2 * r + j]
                        tr = nc.tensor.transpose(PS[:, 1 + r % 3, 256 * j + 128 * t:256 * j + 128 * t + 128],
                                                 P2[:, t, c0:c0 + 128], IDENT)
                tr.then_inc(S("qk2_turned"), 1)
            pe.wait_ge(S("qk2_copied"), 10)
            pe.wait_ge(S("bias_b_made"), BH)

            def score(h):
                q, k, p, _ = head_tiles(h)
                if h >= 2:
                    pe.wait_ge(S("logits_made"), h - 1)
                o = PS[:, h % 2, :]
                nc.tensor.matmul(o[:, 0:128], QKT[p:p + 64, q, 0:128], QKT[p:p + 64, k, 0:128], start=True, stop=True)
                nc.tensor.matmul(o[:, 128:384], QKT[p:p + 64, q, 128:256], QKT[p:p + 64, k, 0:256], start=True,
                                 stop=True).then_inc(S("scored"), 1)

            def turn(h):
                pe.wait_ge(S("exped"), h + 1)
                if h >= 2:
                    pe.wait_ge(S("pt_copied"), h - 1)
                for j in range(3):
                    tr = nc.tensor.transpose(PS[:, 2 + h % 2, 128 * j:128 * j + 128], ER[:, h % 3, 128 * j:128 * j + 128],
                                             IDENT)
                tr.then_inc(S("p_turned"), 1)

            def value(h):
                v = head_tiles(h)[3]
                pe.wait_ge(S("pt_copied"), h + 1)
                if h >= 2:
                    pe.wait_ge(S("heads_out"), h - 1)
                o = PS[:, 4 + h % 2, :]
                pt = PTR[:, h % 3, :]
                nc.tensor.matmul(o[:, 0:64], pt[:, 0:128], P2[:, 0, v:v + 64], start=True, stop=True)
                nc.tensor.matmul(o[:, 64:128], pt[:, 128:256], P2[:, 0, v:v + 64], start=True, stop=False)
                nc.tensor.matmul(o[:, 64:128], pt[:, 256:384], P2[:, 1, v:v + 64], start=False, stop=True).then_inc(
                    S("valued"), 1)
            for h in range(SH + 3):
                if h < SH:
                    score(h)
                if 2 <= h <= SH + 1:
                    turn(h - 2)
                if h >= 3:
                    value(h - 3)
            pe.wait_ge(S("heads_out"), SH)
            for j, c0 in enumerate((QC, KC)):
                for t in range(TT):
                    for h in range(CH2):
                        tr = nc.tensor.transpose(PS[0:CK, 2 * j + t, 128 * h:128 * h + 128],
                                                 P2[:, t, c0 + CK * h:c0 + CK * h + CK], IDENT)
            for t in range(TT):
                tr = nc.tensor.transpose(PS[0:16, 4, 128 * t:128 * t + 128], P2[:, t, GL:GL + 16], IDENT)
            tr.then_inc(S("c_turned"), 1)
            pe.wait_ge(S("glt_copied"), 1)
            pe.wait_ge(S("w2_in"), 16)
            for h in range(CH2):
                mm = nc.tensor.matmul(PS[0:CK, 6 + h // 2, 256 * (h % 2):256 * (h % 2) + 256], W2[:, CK * h:CK * h + CK],
                                      GLT, start=True, stop=True)
            mm.then_inc(S("c_gate_ready"), 1)
            GA.pe(pe)
            pe_split(pe, "mix2", OR, ready=(S("mix2_ready"), 1))

        def act_mix2(act):
            act.wait_ge(S("f_args"), 1)
            act.activation(GATES[:, 1, :], GATES[:, 1, :], ACT.Exp, scale=-1.0).then_inc(S("f_exps"), 1)
            act.wait_ge(S("f_exps"), 1)
            act.activation(GATES[:, 1, :], GATES[:, 1, :], ACT.Ln, bias=ONE_COL).then_inc(S("f_exps"), 1)
            for r in range(10):
                act.wait_ge(S("qk2_turned"), r + 1)
                act.activation(QKT[:, 2 * r:2 * r + 2, :].rearrange("p j t -> p (j t)"), PS[:, 1 + r % 3, :],
                               ACT.Copy).then_inc(S("qk2_copied"), 1)

            def expo(h):
                act.wait_ge(S("maxed"), h + 1)
                for t, (c0, c1) in enumerate(((0, 128), (128, 384))):
                    m = 2 * (h % 4) + t
                    last = act.activation(ER[:, h % 3, c0:c1], ER[:, h % 3, c0:c1], ACT.Exp, bias=MAXES[:, m:m + 1],
                                          accum_out=SUMS[:, m:m + 1])
                last.then_inc(S("exped"), 1)

            def ptcopy(h):
                act.wait_ge(S("p_turned"), h + 1)
                if h >= 3:
                    act.wait_ge(S("valued"), h - 2)
                act.activation(PTR[:, h % 3, :], PS[:, 2 + h % 2, 0:384], ACT.Copy).then_inc(S("pt_copied"), 1)
            for h in range(SH + 2):
                if h >= 2:
                    ptcopy(h - 2)
                if h < SH:
                    expo(h)
            act.wait_ge(S("c_turned"), 1)
            act.activation(GLT, PS[0:16, 4, 0:256], ACT.Copy).then_inc(S("glt_copied"), 1)
            act.activation(CQT.rearrange("p t n -> p (t n)"), PS[0:CK, 0:2, :].rearrange("p b n -> p (b n)"), ACT.Copy,
                           scale=CK ** -0.5)
            act.activation(CKT.rearrange("p t n -> p (t n)"), PS[0:CK, 2:4, :].rearrange("p b n -> p (b n)"),
                           ACT.Copy).then_inc(S("c_qk"), 1)
            act.wait_ge(S("c_args"), 1)
            act.activation(CE, CE, ACT.Exp, scale=-1.0).then_inc(S("c_exps"), 1)
            act.wait_ge(S("c_exps"), 1)
            act.activation(CE, CE, ACT.Ln, bias=ONE_COL[0:CK, :]).then_inc(S("c_exps"), 1)
            GA.act(act)
            for t in range(TT):
                act.activation(P2[:, t, 768:1536], P2[:, t, RC:RC + 768], ACT.Silu).then_inc(S("gla_gate"), 1)
            act_split(act, "mix2", LH2)

        def log_sigmoid_args(dve, link, x, neg, ab):
            link(dve.tensor_scalar(neg, x, -1.0, None, ALU.mult))
            link(dve.tensor_tensor(ab, x, neg, ALU.max))

        def dve_mix2(dve):
            link = Chain(dve)
            dve_y_whole(dve, "mix2")
            g = [GATES[:, j, :] for j in range(10)]
            g3 = [x.rearrange("p (t h) -> p t h", t=TT) for x in g]
            link(dve.tensor_tensor(g3[0], P2[:, :, FL:FL + BH], ROWS[:, 272:280].unsqueeze(1).to_broadcast([128, TT, BH]),
                                   ALU.add))
            log_sigmoid_args(dve, link, g[0], g[2], g[1])
            dve.tensor_scalar(g[0], g[0], 0.0, None, ALU.min).then_inc(S("f_args"), 1)
            dve.wait_ge(S("f_args"), 1)
            dve.wait_ge(S("f_exps"), 2)
            dve.tensor_tensor(g[0], g[0], g[1], ALU.subtract).then_inc(S("f_ready"), 1)
            dve.wait_ge(S("c_ready"), 1)
            link(dve.tensor_copy(g[3], PS[:, 0, 0:16]))
            dve.wait_ge(S("c_ready"), 2)
            for h in range(BH):
                cs = PS[:, 4 + h // 2, 256 * (h % 2):256 * (h % 2) + 256]
                dve.tensor_scalar(BIASB[:, h, 0:128], cs[:, 0:128], g[3][:, h:h + 1], -1.0, ALU.subtract, ALU.mult)
                last = dve.tensor_scalar(BIASB[:, h, 128:384], cs, g[3][:, 8 + h:9 + h], -1.0, ALU.subtract, ALU.mult)
            link(last)
            for h in range(BH):
                dve.tensor_tensor(BIASB[:, h, 0:128], BIASB[:, h, 0:128], CAUSAL, ALU.add)
                last = dve.tensor_tensor(BIASB[:, h, 256:384], BIASB[:, h, 256:384], CAUSAL, ALU.add)
                last.then_inc(S("bias_b_made"), 1)
            dve.wait_ge(S("bias_b_made"), BH)
            dve.wait_ge(S("bias_a_in"), 16 * AH)

            def logits(h):
                dve.wait_ge(S("scored"), h + 1)
                if h >= 3:
                    dve.wait_ge(S("p_turned"), h - 2)
                else:
                    dve.wait_ge(S("qk2_turned"), 10)
                e, ps = ER[:, h % 3, :], PS[:, h % 2, :]
                b0, b1 = (BIASA[:, h, 128:256], BIASA[:, h, :]) if h < AH else \
                    (BIASB[:, h - AH, 0:128], BIASB[:, h - AH, 128:384])
                dve.scalar_tensor_tensor(out=e[:, 0:128], in0=ps[:, 0:128], scalar=HD ** -0.5, in1=b0, op0=ALU.mult,
                                         op1=ALU.add)
                dve.scalar_tensor_tensor(out=e[:, 128:384], in0=ps[:, 128:384], scalar=HD ** -0.5, in1=b1, op0=ALU.mult,
                                         op1=ALU.add).then_inc(S("logits_made"), 1)
                dve.wait_ge(S("logits_made"), h + 1)
                m = 2 * (h % 4)
                dve.tensor_reduce(MAXES[:, m:m + 1], e[:, 0:128], AX, ALU.max)
                link(dve.tensor_reduce(MAXES[:, m + 1:m + 2], e[:, 128:384], AX, ALU.max))
                dve.tensor_scalar(MAXES[:, m:m + 2], MAXES[:, m:m + 2], -1.0, None, ALU.mult).then_inc(S("maxed"), 1)

            def output(h):
                dve.wait_ge(S("valued"), h + 1)
                m = 2 * (h % 4)
                link(dve.reciprocal(SUMS[:, m:m + 2], SUMS[:, m:m + 2]))
                for t in range(TT):
                    last = dve.tensor_scalar(OR[:, t, HD * h:HD * h + HD], PS[:, 4 + h % 2, 64 * t:64 * t + 64],
                                             SUMS[:, m + t:m + t + 1], None, ALU.mult)
                last.then_inc(S("heads_out"), 1)
            for h in range(SH + 3):
                if h >= 3:
                    output(h - 3)
                if h < SH:
                    logits(h)
            dve.wait_ge(S("c_gate_ready"), 1)
            for h in range(CH2):
                hs = slice(128 * h, 128 * h + 128)
                last = dve.tensor_scalar(CX[:, :, hs],
                                         PS[0:CK, 6 + h // 2, 256 * (h % 2):256 * (h % 2) + 256].rearrange(
                                             "p (t n) -> p t n", t=TT), COLS[0:CK, 214 + h:215 + h], None, ALU.add)
            link(last)
            log_sigmoid_args(dve, link, CX, CE, CE)
            dve.tensor_scalar(CX, CX, 0.0, None, ALU.min).then_inc(S("c_args"), 1)
            dve.wait_ge(S("c_args"), 1)
            dve.wait_ge(S("c_exps"), 2)
            link(dve.tensor_tensor(CX, CX, CE, ALU.subtract))
            link(dve.tensor_scalar(CX, CX, 1.0 / 16.0, None, ALU.mult))
            cx, cb = (x.rearrange("p t n -> p (t n)") for x in (CX, CBT))
            for j in range(TT * CH2 * 128 // CH):
                js = slice(CH * j, CH * j + CH)
                last = dve.tensor_tensor_scan(out=cb[:, js], data0=ONES[0:CK, 0:CH], data1=cx[:, js], initial=0.0,
                                              op0=ALU.mult, op1=ALU.add)
            link(last)
            dve.wait_ge(S("c_qk"), 1)
            link(dve.memset(CKM, 0.0))
            link(dve.memset(CQM, 0.0))
            GA.dve(dve)
            dve.wait_ge(S("decay_outputs"), 2)
            for t in range(TT):
                for j in range(2):
                    last = dve.tensor_copy(OR[:, t, 1280 + 384 * j:1280 + 384 * j + 384], PS[:, 2 * t + j, 0:384])
            link(last)
            dve.wait_ge(S("gla_gate"), 2)

            def c4(x, c0):
                return [x[:, t, c0:c0 + 768].rearrange("p (h n) -> p h n", h=CH2) for t in range(TT)]
            dve_heads(dve, link, "gla_heads", c4(OR, 1280), c4(P2, 0), c4(P2, 768), ROWS[:, 296:296 + CV],
                      CH2, CV, CSTAT).then_inc(S("mix2_ready"), 1)
            dve_split(dve, "mix2", LH2, LL2)

        (_, _, _, _, MEMR) = region(*[(f"m{j}", [128, KT, T], F32R) for j in range(2)], ("m2", [128, TT, D], F32),
                                    ("m3", [128, TT, D], F32), ("memory_rows", [128, TT, D], F32))

        def pool_norm_mem(pool):
            pool.wait_ge(S("mix2_ready"), 1)
            pool.dma_start(MEMR[:, :, :], a["mem_2"].rearrange("(t p) d -> p t d", p=128)).then_inc(S("mem_in"), 16)
            pool.dma_start(VEC[:, :], row_vector("mem_norm_2")).then_inc(S("vecs_in"), 16)
            pool.dma_start(VEC2, row_vector("norm_cross_2")).then_inc(S("vecs_in"), 16)
            pool_rstd(pool, "mem")
            pool_rstd(pool, "cross_in")

        def act_norm_mem(act):
            act_squares(act, "mem", MEMR)
            act_split(act, "norm_mem", LH2)
            act.wait_ge(S("round_free"), round_of["norm_mem"] + 8)
            act_squares(act, "cross_in", X)

        def pe_norm_mem(pe):
            pe_split(pe, "norm_mem", MEMR, ready=(S("h_ready"), 7))

        def dve_norm_mem(dve):
            link = Chain(dve)
            dve.wait_ge(S("mem_in"), 16)
            dve_rows_ready(dve)
            dve.wait_ge(S("vecs_in"), 96)
            dve_norm_rows(dve, link, "mem", MEMR, MEMR, VEC[:, :])
            dve_split(dve, "norm_mem", LH2, LL2)
            dve_y_whole(dve, "norm_mem")
            dve_rows_ready(dve)
            dve_norm_rows(dve, link, "cross_in", Y, X, VEC2)

        def act_norm_cross(act):
            act_split(act, "norm_cross", LH2)

        def pe_norm_cross(pe):
            pe_split(pe, "norm_cross", Y, ready=(S("h_ready"), 9))

        def dve_norm_cross(dve):
            dve_split(dve, "norm_cross", LH2, LL2)

        YF = Y[:, :, :].rearrange("p t d -> p (t d)")
        XQT = YF[:, 0:1024].rearrange("p (h t) -> p h t", h=XH)
        XKT = YF[:, 1024:2048].rearrange("p (h t) -> p h t", h=XH)
        XE = YF[:, 2048:3072].rearrange("p (r x) -> p r x", r=2)
        XP = YF[:, 3072:4096].rearrange("p (r x) -> p r x", r=2)
        XO = NAT[:, :, 0:XH * XD]
        XMAX, XSUM = SM[:, 152:160], SM[:, 160:168]

        def pe_cross(pe):
            for b in range(4):
                pe.wait_ge(S(f"bank_free{b}"), AT["cross"]["done"][b])
            for j, src in enumerate((QX, KV)):
                for h in range(XH):
                    for t in range(TT):
                        tr = nc.tensor.transpose(PS[:, 2 * j + h // 2, 256 * (h % 2) + 128 * t:256 * (h % 2) + 128 * t + 128],
                                                 src[:, t, 128 * h:128 * h + 128], IDENT)
                tr.then_inc(S("x_turned"), 1)
            pe.wait_ge(S("x_copied"), 2)

            def score(h):
                if h >= 2:
                    pe.wait_ge(S("x_exped"), h - 1)
                for t in range(TT):
                    mm = nc.tensor.matmul(PS[:, 4 + h % 2, 256 * t:256 * t + 256], XQT[:, h, 128 * t:128 * t + 128],
                                          XKT[:, h, :], start=True, stop=True)
                mm.then_inc(S("x_scored"), 1)

            def turn(h):
                pe.wait_ge(S("x_exped"), h + 1)
                if h >= 2:
                    pe.wait_ge(S("xp_copied"), h - 1)
                for t in range(TT):
                    for s in range(TT):
                        c0 = 256 * t + 128 * s
                        tr = nc.tensor.transpose(PS[:, 6 + h % 2, c0:c0 + 128], XE[:, h % 2, c0:c0 + 128], IDENT)
                tr.then_inc(S("xp_turned"), 1)

            def value(h):
                pe.wait_ge(S("xp_copied"), h + 1)
                if h >= 2:
                    pe.wait_ge(S("x_out"), h - 1)
                for t in range(TT):
                    for s in range(TT):
                        mm = nc.tensor.matmul(PS[:, h % 2, 128 * t:128 * t + 128],
                                              XP[:, h % 2, 256 * t + 128 * s:256 * t + 128 * s + 128],
                                              KV[:, s, 512 + 128 * h:512 + 128 * h + 128], start=(s == 0), stop=(s == 1))
                mm.then_inc(S("x_valued"), 1)
            for h in range(XH + 2):
                if h < XH:
                    score(h)
                if 1 <= h <= XH:
                    turn(h - 1)
                if h >= 2:
                    value(h - 2)
            pe_split(pe, "cross", XO, 4, ready=(S("x_out"), XH))

        def act_cross(act):
            act.wait_ge(S("x_turned"), 1)
            act.activation(XQT.rearrange("p h t -> p (h t)"), bank_cols(0, 2), ACT.Copy)
            act.wait_ge(S("x_turned"), 2)
            act.activation(XKT.rearrange("p h t -> p (h t)"), bank_cols(2, 2), ACT.Copy).then_inc(S("x_copied"), 2)

            def expo(h):
                act.wait_ge(S("x_maxed"), h + 1)
                if h >= 2:
                    act.wait_ge(S("xp_turned"), h - 1)
                for t in range(TT):
                    m = 2 * h + t
                    last = act.activation(XE[:, h % 2, 256 * t:256 * t + 256], PS[:, 4 + h % 2, 256 * t:256 * t + 256],
                                          ACT.Exp, bias=XMAX[:, m:m + 1], scale=XD ** -0.5, accum_out=XSUM[:, m:m + 1])
                last.then_inc(S("x_exped"), 1)

            def pcopy(h):
                act.wait_ge(S("xp_turned"), h + 1)
                if h >= 2:
                    act.wait_ge(S("x_valued"), h - 1)
                act.activation(XP[:, h % 2, :], PS[:, 6 + h % 2, :], ACT.Copy).then_inc(S("xp_copied"), 1)
            for h in range(XH + 1):
                if h < XH:
                    expo(h)
                if h >= 1:
                    pcopy(h - 1)
            act_split(act, "cross", LH2, 4)

        def dve_cross(dve):
            link = Chain(dve)

            def maxes(h):
                dve.wait_ge(S("x_scored"), h + 1)
                link(dve.tensor_reduce(XMAX[:, 2 * h:2 * h + 2],
                                       PS[:, 4 + h % 2, :].rearrange("p (t s) -> p t s", t=TT), AX, ALU.max))
                dve.tensor_scalar(XMAX[:, 2 * h:2 * h + 2], XMAX[:, 2 * h:2 * h + 2], -XD ** -0.5, None,
                                  ALU.mult).then_inc(S("x_maxed"), 1)

            def output(h):
                dve.wait_ge(S("x_valued"), h + 1)
                link(dve.reciprocal(XSUM[:, 2 * h:2 * h + 2], XSUM[:, 2 * h:2 * h + 2]))
                for t in range(TT):
                    last = dve.tensor_scalar(XO[:, t, 128 * h:128 * h + 128], PS[:, h % 2, 128 * t:128 * t + 128],
                                             XSUM[:, 2 * h + t:2 * h + t + 1], None, ALU.mult)
                last.then_inc(S("x_out"), 1)
            for h in range(XH + 2):
                if h < XH:
                    maxes(h)
                if h >= 2:
                    output(h - 2)
            dve_split(dve, "cross", LH2, LL2, 4)

        def pool_norm_ffn2(pool):
            pool.wait_ge(S("h_ready"), 7)
            pool.dma_start(VEC[:, :], row_vector("norm_ffn_2")).then_inc(S("vecs_in"), 16)
            pool_rstd(pool, "ffn2_in")
            pool.wait_ge(S("h_ready"), 11)
            pool.dma_start(VEC[:, :], row_vector("norm_final_2")).then_inc(S("vecs_in"), 16)

        def act_norm_ffn2(act):
            act_squares(act, "ffn2_in", X)
            act_split(act, "norm_ffn2", LH2)

        def pe_norm_ffn2(pe):
            pe_split(pe, "norm_ffn2", Y, ready=(S("h_ready"), 11))

        def dve_norm_ffn2(dve):
            link = Chain(dve)
            dve_y_whole(dve, "norm_ffn2")
            dve_rows_ready(dve)
            dve.wait_ge(S("vecs_in"), 112)
            dve_norm_rows(dve, link, "ffn2_in", Y, X, VEC[:, :])
            dve_split(dve, "norm_ffn2", LH2, LL2)

        GT = MOD[:, 2, :].rearrange("p (k t) -> p k t", k=8)
        turns2 = [c for _, cs in segs for c in cs if c.phase == "hid2"]
        for c, n in zip(turns2, (0, 1, 4)):
            HID[id(c)] = n
        waits2 = [c for _, cs in segs for c in cs if c.phase == "hid_wait" and c.w is a["w_down_2"]]
        LOWS_BEFORE = {}
        for c, n in zip(waits2, (0, 3, 4)):
            LOWS_BEFORE[id(c)] = 4 * n + 4

        def hid2_step(j, nk, last_j=7):
            q = j // 2

            def turn_no(c, i):
                return (HID[id(c)] if c is not None else 5), (i is not None)

            def pe_f(pe, c=None, i=None):
                n, looped = turn_no(c, i)
                pe_round(pe, round_of["hid2"] + 8 * n + j, NATV if j % 2 else NATG, 2 * q, nk, i, 8 if looped else 0)

            def act_f(act, c=None, i=None):
                n, looped = turn_no(c, i)
                rd = round_of["hid2"] + 8 * n + j
                act.wait_ge(S("round_free"), val(rd + 1, 8 if looped else 0, i))
                dst, func, done = ((GT, ACT.Silu, "gate_silu"), (L2H, ACT.Copy, "hid_high2"))[j % 2]
                act.activation(dst[:, 2 * q:2 * q + nk, :], GT[:, 2 * q:2 * q + nk, :], func).then_inc(S(done), 1)

            def low(dve, n, looped, i, q, nk):
                dve.wait_ge(S("hid_high2"), val(4 * n + q + 1, 4 if looped else 0, i))
                dve.tensor_tensor(L2L[:, 2 * q:2 * q + nk, :], GT[:, 2 * q:2 * q + nk, :],
                                  L2H[:, 2 * q:2 * q + nk, :].bitcast(F32), ALU.subtract).then_inc(S("hid_low2"), 1)

            def dve_f(dve, c=None, i=None):
                n, looped = turn_no(c, i)
                seen, step = 4 * n + q + 1, 4 if looped else 0
                rd = round_of["hid2"] + 8 * n + j
                if j % 2 == 0 and q:
                    low(dve, n, looped, i, q - 1, 2)
                dve.wait_ge(S("round_ready"), val(rd + 1, 8 if looped else 0, i))
                bank = PS[:, 4 + rd % 4, :].rearrange("p (k t) -> p k t", k=2)
                if j % 2 == 0:
                    if n:
                        dve.wait_ge(S("hid_low2"), val(seen - 4, step, i))
                    for tap in (2, 1, 0):
                        for k in range(nk):
                            kt = 2 * q + k
                            sh = 2 - tap
                            wcol = conv_col(tap, n, looped, i, kt)
                            src, dst = bank[:, k, 0:T - sh], GT[:, kt, sh:T]
                            if sh == 0:
                                last = dve.tensor_scalar(dst, src, wcol, conv_col(3, n, looped, i, kt), ALU.mult, ALU.add)
                            else:
                                last = dve.scalar_tensor_tensor(out=dst, in0=src, scalar=wcol, in1=dst, op0=ALU.mult,
                                                                op1=ALU.add)
                        if tap:
                            last.then_inc(S("tap_done"), 1)
                            taps = 2 * (4 * n + q) + 3 - tap
                            dve.wait_ge(S("tap_done"), val(taps, 8 if looped else 0, i))
                    last.then_inc(S("round_free"), 1)
                else:
                    dve.wait_ge(S("gate_silu"), val(seen, step, i))
                    g = GT[:, 2 * q:2 * q + nk, :]
                    dve.tensor_tensor(g, g, bank[:, 0:nk, :], ALU.mult).then_inc(S("round_free"), 1)
                    if j == last_j:
                        low(dve, n, looped, i, q, nk)
            return pe_f, act_f, dve_f

        def conv_col(tap, n, looped, i, kt):
            base = (128, 171, 256, 299)[tap] + 8 * n + kt
            if looped:
                return COLS[:, ds(i * 8 + base, 1)]
            return COLS[:, base:base + 1]

        steps = [hid2_step(j, 2) for j in range(8)]
        AT_UNIT = (0, 2, 4, 6, 8, 10, 12, 13)

        def spread(n):
            return [steps[AT_UNIT.index(k)][n] if k in AT_UNIT else None for k in range(KT)]
        hid2 = dict(pe=spread(0), act=spread(1), dve=spread(2))
        last_steps = [hid2_step(j, 2 if j < 2 else 1, 3) for j in range(4)]

        def all_of(n):
            def f(eng):
                for s in last_steps:
                    s[n](eng)
            return f

        def pe_hid2_last(pe):
            all_of(0)(pe)
            pe.wait_ge(S("hid_low2"), 22)
        hid2_last = dict(pe=[pe_hid2_last], act=[all_of(1)], dve=[all_of(2)])

        def wait_hidden(pe, c, i):
            if c.w is a["w_ff2"]:
                wait_hid(pe, c, i)
            else:
                pe.wait_ge(S("hid_low2"), val(LOWS_BEFORE[id(c)], 4 if i is not None else 0, i))

        phases = [("norm_in", dict(pe=[pe_norm_in], act=[act_norm_in], dve=[dve_norm_in])),
                  ("conv0", conv_fns(0)), ("conv1", conv_fns(1)), ("conv2", conv_fns(2)),
                  ("mix1", dict(pe=[pe_mix1], act=[None, act_mix1], dve=[None, dve_mix1])),
                  ("norm_ffn1", dict(pe=[pe_norm_ffn1], act=[act_norm_ffn1], dve=[dve_norm_ffn1])),
                  ("hid1", hid1_fns(4)), ("hid_wait", dict(pe=[wait_hidden])), ("hid1_last", last_hid1()),
                  ("norm_in2", dict(pe=[pe_norm_in2], act=[act_norm_in2], dve=[dve_norm_in2])),
                  ("mix2", dict(pe=[pe_mix2], act=[act_mix2], dve=[dve_mix2])),
                  ("norm_mem", dict(pe=[pe_norm_mem], act=[act_norm_mem], dve=[dve_norm_mem])),
                  ("norm_cross", dict(pe=[pe_norm_cross], act=[act_norm_cross], dve=[dve_norm_cross])),
                  ("cross", dict(pe=[pe_cross], act=[act_cross], dve=[dve_cross])),
                  ("norm_ffn2", dict(pe=[pe_norm_ffn2], act=[act_norm_ffn2], dve=[dve_norm_ffn2])),
                  ("hid2", hid2), ("hid2_last", hid2_last)]
        POOL = {"mix1": pool_mix1, "norm_ffn1": pool_norm_ffn1, "norm_in2": pool_norm_in2, "mix2": pool_mix2,
                "norm_mem": pool_norm_mem, "norm_ffn2": pool_norm_ffn2}
        pool_order = list(POOL)

        def act_end(act):
            act_squares(act, "final", X)

        def dve_end(dve):
            link = Chain(dve)
            dve_evac(dve, TAIL, None)
            for b in range(4):
                dve.wait_ge(S(f"bank_free{b}"), TAIL.at["done"][b])
            dve_rows_ready(dve)
            dve.wait_ge(S("vecs_in"), 128)
            dve_norm_rows(dve, link, "final", Y, X, VEC[:, :])

        def pool_end(pool):
            pool_rstd(pool, "final")
            for t in range(TT):
                pool.wait_ge(S("h_ready"), 12 + t)
                pool.dma_start(out[128 * t:128 * t + 128, :], Y[:, t, :]).then_inc(S("out_written"), 16)
            pool.wait_ge(S("out_written"), 32)

        PHASES = dict(phases)

        def hooks_for(which, eng):
            def run(c, j, i):
                if not c.phase or c.phase == "none":
                    return
                fns = PHASES[c.phase].get(which, [])
                if j < len(fns) and fns[j]:
                    fns[j](eng, *(() if c.phase not in TURNED and c.phase != "hid_wait" else (c, i)))
            return run

        def stream(chunk_fn, eng, *more):
            for iters, chunks in segs:
                if iters == 1:
                    for c in chunks:
                        chunk_fn(eng, c, None, *more)
                else:
                    with eng.Fori(0, iters) as i:
                        for c in chunks:
                            chunk_fn(eng, c, i, *more)

        block = ctx.enter_context(nc.Block())

        @block.sync
        def _(sp):
            sp_ada_first(sp)
            stream(sp_chunk, sp)

        @block.scalar
        def _(act):
            act_start(act)
            stream(act_chunk, act, hooks_for("act", act), act_evac)
            act_end(act)

        @block.vector
        def _(dve):
            dve_start(dve)
            stream(dve_chunk, dve, hooks_for("dve", dve), dve_evac)
            dve_end(dve)

        @block.tensor
        def _(pe):
            pe_start(pe)
            stream(pe_chunk, pe, hooks_for("pe", pe))

        @block.gpsimd
        def _(pool):
            pool_start(pool)
            for name in pool_order:
                POOL[name](pool)
            pool_end(pool)


_INS = ["x", "c", "w_ada", "b_ada", "pre_mix_norm", "post_mix_norm", "pre_ffn_norm", "post_ffn_norm", "w_in",
        "hg_lb_logits", "hg_norm", "gdn_conv_w", "gdn_a_log", "gdn_dt_bias", "gdn_norm", "w_out", "w_ff1", "w_ff2",
        "mem_2", "rel_table_2", "mem_norm_2", "norm_final_2", "norm_mix_2", "w_in_2", "f_bias_2", "c_gate_w2_2",
        "c_gate_b_2", "c_norm_2", "w_out_2", "norm_cross_2", "w_cq_2", "w_ckv_2", "w_co_2", "norm_ffn_2", "w_up_2",
        "conv_w_2", "conv_b_2", "w_down_2"]
_WHOLE = ("hg_lb_logits", "rel_table_2", "c", "mem_norm_2", "norm_final_2")


def kernel(**inputs):
    import numpy as _np
    import concourse.bacc as _bacc
    from concourse import mybir as _mybir
    from concourse.bass_utils import run_bass_kernel_spmd as _run

    nc = _bacc.Bacc("TRN2", target_bir_lowering=False, num_devices=1)
    arrays, aps = {}, {}

    def add(name, array):
        arrays[f"in_{name}"] = _np.ascontiguousarray(array)
        aps[name] = nc.dram_tensor(f"in_{name}", arrays[f"in_{name}"].shape, _mybir.dt.from_np(array.dtype),
                                   kind="ExternalInput").ap()

    for name in _INS:
        array = _np.asarray(inputs[name])
        add(name, array if name in _WHOLE else array[0])
    for name, table in zip(("table_f", "table_m", "distances"), shape_constants()):
        add(name, table)
    out = nc.dram_tensor("out_0", OUT_SHAPE, _mybir.dt.float32, kind="ExternalOutput").ap()
    aps["toeplitz"] = nc.dram_tensor("toeplitz", (AH, 128, 384), _mybir.dt.float32, kind="Internal").ap()
    block_pair(nc, aps, out, STOP)
    r = _run(nc, [arrays], core_ids=[0])
    return r.results[0]["out_0"].reshape(OUT_RESHAPE)
STOP = None
OUT_SHAPE = (256, 2048)
OUT_RESHAPE = (1, 256, 2048)
```
